# Optimizing a Trainium2 kernel written in Bass

```python
import math, functools
import jax, jax.numpy as jnp
from jax import lax
import numpy as np

D_MODEL = 1024
BATCH = 1
SEQ = 1024
DEPTH = 1
DEC_BATCH = 8
DEC_SEQ = 8
PAST_LEN = 8192
PAGE_SIZE = 128

N_META = 16
DN_HEADS = 16
DN_HEAD_K = 64
DN_HEAD_V = 64
DN_QK_DIM = DN_HEADS * DN_HEAD_K
DN_V_DIM = DN_HEADS * DN_HEAD_V
DN_QKV_DIM = 2 * DN_QK_DIM + DN_V_DIM
SSM_HEADS = 16
SSM_HEAD_DIM = 64
SSM_GROUPS = 2
SSM_STATE = 128
D_SSM = SSM_HEADS * SSM_HEAD_DIM
SSM_XBC_DIM = D_SSM + 2 * SSM_GROUPS * SSM_STATE
D_MIX = DN_V_DIM + D_SSM
PROJ_DIM = DN_QKV_DIM + DN_V_DIM + 2 * DN_HEADS + D_SSM + SSM_XBC_DIM + SSM_HEADS
CONV_K = 4
CHUNK = 64
PEER_HEADS = 8
N_KEYS = 128
N_EXPERTS = N_KEYS * N_KEYS
D_KEY = 256
TOP_K = 16
PEER_BLOCK = 128
ALPHA = (2 * DEPTH) ** 0.25
BETA_INIT = (8 * DEPTH) ** -0.25

kernel_name = 'hymba_gdn_ssd_peer_step'

def layer_norm(x, g, b, eps=1e-5):
    xf = x.astype(jnp.float32)
    mu = jnp.mean(xf, axis=-1, keepdims=True)
    var = jnp.mean(jnp.square(xf - mu), axis=-1, keepdims=True)
    return ((xf - mu) * lax.rsqrt(var + eps) * g.astype(jnp.float32) + b.astype(jnp.float32)).astype(x.dtype)

def rms_norm(x, g, eps=1e-6):
    xf = x.astype(jnp.float32)
    return (xf * lax.rsqrt(jnp.mean(jnp.square(xf), -1, keepdims=True) + eps) * g.astype(jnp.float32)).astype(x.dtype)

def l2_normalize(x, eps=1e-6):
    xf = x.astype(jnp.float32)
    return (xf * lax.rsqrt(jnp.sum(jnp.square(xf), -1, keepdims=True) + eps)).astype(x.dtype)

def causal_conv(x, prev, w, b=None):
    k_width, length = w.shape[0], x.shape[1]
    xp = jnp.concatenate([prev.astype(x.dtype), x], axis=1)
    y = sum(w[i] * xp[:, i:i + length] for i in range(k_width))
    if b is not None:
        y = y + b
    return y, xp[:, length:]

def gated_delta_chunked(q, k, v, g, beta, s0, chunk):
    bsz, length, heads, _ = q.shape
    dv = v.shape[-1]
    n = length // chunk

    def to_chunks(a):
        a = a.astype(jnp.float32).reshape(bsz, n, chunk, heads, *a.shape[3:])
        return jnp.moveaxis(a, (1, 3), (0, 2))

    causal = jnp.tril(jnp.ones((chunk, chunk), bool))
    strict = jnp.tril(jnp.ones((chunk, chunk), bool), -1)
    eye = jnp.eye(chunk, dtype=jnp.float32)

    def body(s, inp):
        qc, kc, vc, gc, bc = inp
        cum = jnp.cumsum(gc, axis=-1)
        decay = jnp.exp(jnp.where(causal, cum[..., :, None] - cum[..., None, :], -jnp.inf))
        kk = jnp.einsum('bhid,bhjd->bhij', kc, kc)
        a_mat = jnp.where(strict, bc[..., :, None] * kk * decay, 0.0)
        rhs = jnp.concatenate([bc[..., None] * vc, (bc * jnp.exp(cum))[..., None] * kc], axis=-1)
        sol = lax.linalg.triangular_solve(a_mat + eye, rhs, left_side=True, lower=True, unit_diagonal=True)
        u, w = sol[..., :dv], sol[..., dv:]
        delta = u - jnp.einsum('bhck,bhkv->bhcv', w, s)
        qk = jnp.where(causal, jnp.einsum('bhid,bhjd->bhij', qc, kc) * decay, 0.0)
        o = jnp.exp(cum)[..., None] * jnp.einsum('bhck,bhkv->bhcv', qc, s) + jnp.einsum('bhij,bhjv->bhiv', qk, delta)
        last = cum[..., -1:]
        s_new = jnp.exp(last)[..., None] * s + jnp.einsum('bhck,bhcv->bhkv', jnp.exp(last - cum)[..., None] * kc, delta)
        return s_new, o

    s_fin, o = lax.scan(body, s0.astype(jnp.float32), tuple(to_chunks(a) for a in (q, k, v, g, beta)))
    o = jnp.moveaxis(o, (0, 2), (1, 3)).reshape(bsz, length, heads, dv)
    return o, s_fin

def ssd_chunked(x, dt, b_in, c_in, h0, chunk, a_neg):
    bsz, length, heads, hdim = x.shape
    groups, nst = b_in.shape[2:]
    rep = heads // groups
    n = length // chunk

    def to_chunks(a):
        return jnp.moveaxis(a.astype(jnp.float32).reshape(bsz, n, chunk, *a.shape[2:]), 1, 0)

    causal = jnp.tril(jnp.ones((chunk, chunk), bool))
    a_g = a_neg.astype(jnp.float32).reshape(groups, rep)

    def body(h, inp):
        xc, dtc, bc, cc = inp
        cum = jnp.cumsum(dtc * a_g, axis=1)
        cum_t = jnp.moveaxis(cum, 1, -1)
        lmat = jnp.exp(jnp.where(causal, cum_t[..., :, None] - cum_t[..., None, :], -jnp.inf))
        cb = jnp.einsum('bign,bjgn->bgij', cc, bc)
        xdt = xc * dtc[..., None]
        y_intra = jnp.einsum('bgrij,bjgrp->bigrp', lmat * cb[:, :, None], xdt)
        y_inter = jnp.exp(cum)[..., None] * jnp.einsum('bign,bgrpn->bigrp', cc, h)
        last = cum[:, -1:]
        h_new = jnp.exp(last[:, 0])[..., None, None] * h + jnp.einsum('bjgrp,bjgn->bgrpn', xdt * jnp.exp(last - cum)[..., None], bc)
        return h_new, y_intra + y_inter

    xs = (x.reshape(bsz, length, groups, rep, hdim), dt.reshape(bsz, length, groups, rep), b_in, c_in)
    h_fin, y = lax.scan(body, h0.astype(jnp.float32).reshape(bsz, groups, rep, hdim, nst), tuple(to_chunks(a) for a in xs))
    y = jnp.moveaxis(y, 0, 1).reshape(bsz, length, heads, hdim)
    return y, h_fin.reshape(bsz, heads, hdim, nst)

def run_segments(chunk_fn, arrays, state, n_lead):
    length = arrays[0].shape[1]
    outs = []
    for start, stop in ((0, n_lead), (n_lead, length)):
        if stop > start:
            o, state = chunk_fn(*(a[:, start:stop] for a in arrays), state, math.gcd(stop - start, CHUNK))
            outs.append(o)
    return jnp.concatenate(outs, axis=1), state

def mixer_sublayer(h, dn_conv_prev, dn_s0, ssm_conv_prev, ssm_h0, n_lead,
                   w_in, dn_conv_w, dn_A_log, dn_dt_bias, dn_norm_g,
                   ssm_conv_w, ssm_conv_b, ssm_A_log, ssm_dt_bias, ssm_D, ssm_norm_g, w_out):
    bsz, length, _ = h.shape
    dtype = h.dtype
    sizes = (DN_QKV_DIM, DN_V_DIM, DN_HEADS, DN_HEADS, D_SSM, SSM_XBC_DIM, SSM_HEADS)
    points = [int(p) for p in np.cumsum(sizes)[:-1]]
    proj = jnp.einsum('bld,de->ble', h, w_in)
    dn_qkv, dn_z, dn_b, dn_a, ssm_z, ssm_xbc, ssm_dt = jnp.split(proj, points, axis=-1)

    qkv, dn_conv_new = causal_conv(dn_qkv, dn_conv_prev, dn_conv_w)
    qkv = jax.nn.silu(qkv)
    q, k, v = jnp.split(qkv, [DN_QK_DIM, 2 * DN_QK_DIM], axis=-1)
    q = l2_normalize(q.reshape(bsz, length, DN_HEADS, DN_HEAD_K)) * (DN_HEAD_K ** -0.5)
    k = l2_normalize(k.reshape(bsz, length, DN_HEADS, DN_HEAD_K))
    v = v.reshape(bsz, length, DN_HEADS, DN_HEAD_V)
    beta = jax.nn.sigmoid(dn_b.astype(jnp.float32))
    g = -jnp.exp(dn_A_log.astype(jnp.float32)) * jax.nn.softplus(dn_a.astype(jnp.float32) + dn_dt_bias.astype(jnp.float32))
    o, dn_s = run_segments(gated_delta_chunked, (q, k, v, g, beta), dn_s0, n_lead)
    o = rms_norm(o.astype(dtype), dn_norm_g) * jax.nn.silu(dn_z.reshape(bsz, length, DN_HEADS, DN_HEAD_V))

    xbc, ssm_conv_new = causal_conv(ssm_xbc, ssm_conv_prev, ssm_conv_w, ssm_conv_b)
    xbc = jax.nn.silu(xbc)
    xs, b_in, c_in = jnp.split(xbc, [D_SSM, D_SSM + SSM_GROUPS * SSM_STATE], axis=-1)
    xs = xs.reshape(bsz, length, SSM_HEADS, SSM_HEAD_DIM)
    b_in = b_in.reshape(bsz, length, SSM_GROUPS, SSM_STATE)
    c_in = c_in.reshape(bsz, length, SSM_GROUPS, SSM_STATE)
    dt = jax.nn.softplus(ssm_dt.astype(jnp.float32) + ssm_dt_bias.astype(jnp.float32))
    a_neg = -jnp.exp(ssm_A_log.astype(jnp.float32))
    y, ssm_h = run_segments(functools.partial(ssd_chunked, a_neg=a_neg), (xs, dt, b_in, c_in), ssm_h0, n_lead)
    y = y.astype(dtype) + ssm_D[:, None] * xs
    y = rms_norm(y.reshape(bsz, length, D_SSM) * jax.nn.silu(ssm_z), ssm_norm_g)

    mixed = jnp.einsum('ble,ed->bld', jnp.concatenate([o.reshape(bsz, length, DN_V_DIM), y], axis=-1), w_out)
    return mixed, (dn_conv_new, dn_s.astype(dtype), ssm_conv_new, ssm_h.astype(dtype))

def peer(x, w_q, keys, u_tab, v_tab):
    n_tok = x.shape[0]
    n_blk = -(-n_tok // PEER_BLOCK)
    xp = jnp.pad(x, ((0, n_blk * PEER_BLOCK - n_tok), (0, 0))).reshape(n_blk, PEER_BLOCK, D_MODEL)

    def block(xb):
        q = jnp.einsum('td,de->te', xb, w_q).reshape(PEER_BLOCK, PEER_HEADS, 2, D_KEY // 2)
        s = jnp.einsum('thcd,hcnd->thcn', q.astype(jnp.float32), keys.astype(jnp.float32))
        sv, si = lax.top_k(s, TOP_K)
        cand = sv[:, :, 0, :, None] + sv[:, :, 1, None, :]
        cv, ci = lax.top_k(cand.reshape(PEER_BLOCK, PEER_HEADS, TOP_K * TOP_K), TOP_K)
        i1 = jnp.take_along_axis(si[:, :, 0], ci // TOP_K, axis=-1)
        i2 = jnp.take_along_axis(si[:, :, 1], ci % TOP_K, axis=-1)
        idx = i1 * N_KEYS + i2
        gate = jax.nn.softmax(cv, axis=-1)
        act = jax.nn.gelu(jnp.einsum('thkd,td->thk', u_tab[idx], xb).astype(jnp.float32), approximate=False)
        return jnp.einsum('thk,thkd->td', (gate * act).astype(xb.dtype), v_tab[idx])

    return lax.map(block, xp).reshape(n_blk * PEER_BLOCK, D_MODEL)[:n_tok]

def setup_inputs(seed: int = 0) -> dict:
    key = jax.random.key(seed)
    ks = iter(jax.random.split(key, 40))

    def nrm(shape, scale):
        return scale * jax.random.normal(next(ks), shape, jnp.float32)

    def dt_bias(shape):
        dt = jnp.exp(jax.random.uniform(next(ks), shape, jnp.float32, math.log(1e-3), math.log(1e-1)))
        return dt + jnp.log(-jnp.expm1(-dt))

    def a_log(shape):
        return jnp.log(jax.random.uniform(next(ks), shape, jnp.float32, 1.0, 16.0))

    def gain(shape):
        return 1.0 + nrm(shape, 0.02)

    L_ = DEPTH
    return {
        'x_prompt': nrm((BATCH, SEQ, D_MODEL), 1.0),
        'x_sample': nrm((DEC_BATCH, DEC_SEQ, D_MODEL), 1.0),
        'state_dn_conv': nrm((L_, DEC_BATCH, CONV_K - 1, DN_QKV_DIM), 1.0),
        'state_dn_rec': nrm((L_, DEC_BATCH, DN_HEADS, DN_HEAD_K, DN_HEAD_V), 0.5),
        'state_ssm_conv': nrm((L_, DEC_BATCH, CONV_K - 1, SSM_XBC_DIM), 1.0),
        'state_ssm_rec': nrm((L_, DEC_BATCH, SSM_HEADS, SSM_HEAD_DIM, SSM_STATE), 0.1),
        'meta_tokens': nrm((N_META, D_MODEL), 1.0),
        'ln_in_g': gain((D_MODEL,)),
        'ln_in_b': nrm((D_MODEL,), 0.02),
        'w_in': nrm((L_, D_MODEL, PROJ_DIM), D_MODEL ** -0.5),
        'dn_conv_w': nrm((L_, CONV_K, DN_QKV_DIM), CONV_K ** -0.5),
        'dn_A_log': a_log((L_, DN_HEADS)),
        'dn_dt_bias': dt_bias((L_, DN_HEADS)),
        'dn_norm_g': gain((L_, DN_HEAD_V)),
        'ssm_conv_w': nrm((L_, CONV_K, SSM_XBC_DIM), CONV_K ** -0.5),
        'ssm_conv_b': nrm((L_, SSM_XBC_DIM), 0.02),
        'ssm_A_log': a_log((L_, SSM_HEADS)),
        'ssm_dt_bias': dt_bias((L_, SSM_HEADS)),
        'ssm_D': gain((L_, SSM_HEADS)),
        'ssm_norm_g': gain((L_, D_SSM)),
        'w_out': nrm((L_, D_MIX, D_MODEL), BETA_INIT * D_MIX ** -0.5),
        'ln1_g': gain((L_, D_MODEL)),
        'ln1_b': nrm((L_, D_MODEL), 0.02),
        'peer_w_q': nrm((L_, D_MODEL, PEER_HEADS * D_KEY), D_MODEL ** -0.5),
        'peer_keys': nrm((L_, PEER_HEADS, 2, N_KEYS, D_KEY // 2), (D_KEY // 2) ** -0.5),
        'peer_u': nrm((L_, N_EXPERTS, D_MODEL), D_MODEL ** -0.5),
        'peer_v': nrm((L_, N_EXPERTS, D_MODEL), BETA_INIT),
        'ln2_g': gain((L_, D_MODEL)),
        'ln2_b': nrm((L_, D_MODEL), 0.02),
    }

def reference(x_prompt, x_sample, state_dn_conv, state_dn_rec, state_ssm_conv, state_ssm_rec,
              meta_tokens, ln_in_g, ln_in_b, w_in, dn_conv_w, dn_A_log, dn_dt_bias, dn_norm_g,
              ssm_conv_w, ssm_conv_b, ssm_A_log, ssm_dt_bias, ssm_D, ssm_norm_g, w_out,
              ln1_g, ln1_b, peer_w_q, peer_keys, peer_u, peer_v, ln2_g, ln2_b):
    dtype = x_prompt.dtype
    bp = x_prompt.shape[0]
    meta = jnp.broadcast_to(meta_tokens.astype(dtype)[None], (bp, N_META, D_MODEL))
    hp = layer_norm(jnp.concatenate([meta, x_prompt], axis=1), ln_in_g, ln_in_b)
    hs = layer_norm(x_sample, ln_in_g, ln_in_b)
    new_p, new_s = [], []
    for l in range(DEPTH):
        lw = (w_in[l], dn_conv_w[l], dn_A_log[l], dn_dt_bias[l], dn_norm_g[l],
              ssm_conv_w[l], ssm_conv_b[l], ssm_A_log[l], ssm_dt_bias[l], ssm_D[l], ssm_norm_g[l], w_out[l])
        zero_p = (jnp.zeros((bp, CONV_K - 1, DN_QKV_DIM), dtype),
                  jnp.zeros((bp, DN_HEADS, DN_HEAD_K, DN_HEAD_V), dtype),
                  jnp.zeros((bp, CONV_K - 1, SSM_XBC_DIM), dtype),
                  jnp.zeros((bp, SSM_HEADS, SSM_HEAD_DIM, SSM_STATE), dtype))
        mix_p, st_p = mixer_sublayer(hp, *zero_p, N_META, *lw)
        mix_s, st_s = mixer_sublayer(hs, state_dn_conv[l], state_dn_rec[l], state_ssm_conv[l], state_ssm_rec[l], 0, *lw)
        new_p.append(st_p)
        new_s.append(st_s)
        hp = layer_norm(ALPHA * hp + mix_p, ln1_g[l], ln1_b[l])
        hs = layer_norm(ALPHA * hs + mix_s, ln1_g[l], ln1_b[l])
        if l == DEPTH - 1:
            hp = hp[:, N_META:]
        n_p = hp.shape[0] * hp.shape[1]
        ff = peer(jnp.concatenate([hp.reshape(-1, D_MODEL), hs.reshape(-1, D_MODEL)], axis=0),
                  peer_w_q[l], peer_keys[l], peer_u[l], peer_v[l])
        hp = layer_norm(ALPHA * hp + ff[:n_p].reshape(hp.shape), ln2_g[l], ln2_b[l])
        hs = layer_norm(ALPHA * hs + ff[n_p:].reshape(hs.shape), ln2_g[l], ln2_b[l])
    new_dn_conv_p = jnp.stack([s[0] for s in new_p], axis=0)
    new_dn_rec_p = jnp.stack([s[1] for s in new_p], axis=0)
    new_ssm_conv_p = jnp.stack([s[2] for s in new_p], axis=0)
    new_ssm_rec_p = jnp.stack([s[3] for s in new_p], axis=0)
    new_dn_conv_s = jnp.stack([s[0] for s in new_s], axis=0)
    new_dn_rec_s = jnp.stack([s[1] for s in new_s], axis=0)
    new_ssm_conv_s = jnp.stack([s[2] for s in new_s], axis=0)
    new_ssm_rec_s = jnp.stack([s[3] for s in new_s], axis=0)
    return (hp, hs, new_dn_conv_p, new_dn_rec_p, new_ssm_conv_p, new_ssm_rec_p,
            new_dn_conv_s, new_dn_rec_s, new_ssm_conv_s, new_ssm_rec_s)


_drawn_inputs = setup_inputs


def setup_inputs(seed=0):
    import zlib

    import numpy as np

    out = dict(_drawn_inputs(seed))
    spreads = {}
    factors = {'dn_norm_g': 3.335, 'ssm_D': 8.986, 'ln2_g': 9.687, 'ln2_b': 8.516, 'ssm_norm_g': 2.686}
    for name, (base, spread) in spreads.items():
        noise = np.random.default_rng([zlib.crc32(name.encode()), seed]).standard_normal(out[name].shape)
        drawn = base * np.exp(spread * noise) if base else spread * noise
        out[name] = __import__('jax').numpy.asarray(drawn.astype(out[name].dtype))
    for name, factor in factors.items():
        out[name] = (out[name] * factor).astype(out[name].dtype)
    return out
```

```python
import numpy as np
import concourse.bass as bass
from concourse import mybir
from contextlib import ExitStack

F32 = mybir.dt.float32
BF16 = mybir.dt.bfloat16
U32 = mybir.dt.uint32
ALU = mybir.AluOpType
ACT = mybir.ActivationFunctionType
AX = mybir.AxisListType.X

P = 128
D = 1024
KT = D // P
SEQ, N_META, DEC_B, DEC_L = 1024, 16, 8, 8
SAMPLE = DEC_B * DEC_L
PACK = SAMPLE + N_META
TOK = PACK + SEQ
TILES = SEQ // P
ROWS = [PACK] + [P] * TILES
COL0 = [0] + [PACK + P * i for i in range(TILES)]
SEGS = DEC_B + 1
H = 16
HD = 64
NST = 128
GROUPS = 2
QKV = 3 * H * HD
XBC = H * HD + 2 * GROUPS * NST
CONV = QKV + XBC
CT = CONV // P
TAPS = 4
CTX = TAPS - 1
SLOT = CTX + DEC_L
SBUF_COLS = DEC_B * SLOT + CTX + N_META + SEQ
CONVW = SBUF_COLS - CTX
PROMPT0 = DEC_B * SLOT
Z = 2 * H * HD
SMALL = 3 * H
PER = 18
NCH = 3
NC_ = TOK // NCH
ZC = 512
NEG = -1.0e30
ALPHA = 2 ** 0.25
LN_EPS, RMS_EPS, L2_EPS = 1e-5, 1e-6, 1e-6
EH, EC, NK, TOPK = 8, 2, 128, 16
SLOTS = EH * TOPK
NEXP = NK * NK
HC = EH * EC
GF = {}
_at = 0
for _n, _w in (("g", 2 * H), ("ncum", 2 * H), ("ecum", 2 * H), ("elast", 2 * H), ("beta", H), ("nbecum", H),
               ("edl", H), ("dt", H), ("dtedl", H)):
    GF[_n] = (_at, _at + _w)
    _at += _w
NG = _at


class Signals:

    def __init__(self, nc, ctx, names, kept=()):
        self.sems = {n: ctx.enter_context(nc.semaphore(n)) for n in names}
        self.sems.update(dict(kept))
        nums = [s.num for s in self.sems.values()]
        self.range = range(min(nums), max(nums) + 1)

    def __getitem__(self, n):
        return self.sems[n]


class Chain:

    def __init__(self, eng, sem):
        self.eng, self.sem, self.n = eng, sem, 0

    def __call__(self, ins):
        self.mark(ins)
        self.sync()

    def mark(self, ins):
        self.n += 1
        ins.then_inc(self.sem, 1)

    def sync(self):
        self.eng.wait_ge(self.sem, self.n)


def bc_last(ap, n):
    return ap.unsqueeze(2).to_broadcast([ap.shape[0], ap.shape[1], n])


def bc_mid(ap, n):
    return ap.unsqueeze(1).to_broadcast([ap.shape[0], n, ap.shape[1]])


def normalize_and_combine_keys(nc, io, hT, wA):
    ctx = ExitStack()
    with ctx:
        sb = lambda n, s, d=F32: ctx.enter_context(nc.sbuf_tensor(n, s, d, allow_name_mangling=True))
        ident = sb("n_ident", [P, P])
        gain, bias = sb("n_gain", [P, D]), sb("n_bias", [P, D])
        x, xn, y = sb("n_x", [P, 3, D]), sb("n_xn", [P, 2, D]), sb("n_y", [P, 3, D])
        stats, mv, rs = sb("n_stats", [P, 2, 2, 6]), sb("n_mv", [P, 2, 2]), sb("n_rs", [P, 2, 2])
        half = sb("n_half", [P, 1])
        wq, keys = sb("n_wq", [P, 3, D]), sb("n_keys", [P, HC, NK])
        wc = sb("n_wc", [P, 2, KT, NK])
        ps = [ctx.enter_context(nc.psum_tensor(f"n_ps{i}", [P, 512], F32)) for i in range(8)]
        S = Signals(nc, ctx, ["n_const", "n_in0", "n_in1", "n_in2", "n_mean", "n_rstd", "n_scaled", "n_gained",
                              "n_ready", "n_tr", "n_evac", "n_st0", "n_st1", "n_st2", "n_v", "n_g", "n_wq0", "n_wq1", "n_wq2",
                              "n_keysin", "n_comb", "n_combevac", "n_wcst0", "n_wcst1", "n_w"])
        NT = TILES + 1
        with nc.Block() as block:
            @block.sync
            def _(sp):
                sp.dma_start(gain[:], io["ln_in_g"][:, :].to_broadcast([P, D])).then_inc(S["n_const"], 16)
                sp.dma_start(bias[:], io["ln_in_b"][:, :].to_broadcast([P, D])).then_inc(S["n_const"], 16)
                sp.dma_start(ident[:], io["ident"][:, :]).then_inc(S["n_const"], 16)
                def store(i):
                    sp.wait_ge(S["n_ready"], i + 1)
                    sp.dma_start(io["h"][i, 0:ROWS[i], :], y[0:ROWS[i], i % 3, :]).then_inc(S[f"n_st{i % 3}"], 16)

                for i in range(NT):
                    if i >= 3:
                        sp.wait_ge(S["n_scaled"], i - 2)
                    sp.dma_start(x[0:ROWS[i], i % 3, :], io["x"][COL0[i]:COL0[i] + ROWS[i], :]).then_inc(
                        S[f"n_in{i % 3}"], 16)
                    if i >= 3:
                        store(i - 3)
                sp.dma_start(wA[:, 0], io["w_in"][:, 0:wA.shape[3]].rearrange("(k p) c -> p k c", p=P)).then_inc(S["n_w"], 16)
                for i in range(NT - 3, NT):
                    store(i)
                for b in range(3):
                    sp.wait_ge(S[f"n_st{b}"], 16 * len(range(b, NT, 3)))
                sp.wait_ge(S["n_w"], 16)

            @block.vector
            def _(v):
                def stats_of(i):
                    R = ROWS[i]
                    v.wait_ge(S[f"n_in{i % 3}"], 16 * (i // 3 + 1))
                    for c in range(2):
                        v.bn_stats(out=stats[0:R, i % 2, c, :], in_=x[0:R, i % 3, c * 512:(c + 1) * 512]).then_inc(S["n_v"], 1)
                    v.wait_ge(S["n_v"], 2 * (i + 1))
                    if i >= 2:
                        v.wait_ge(S["n_rstd"], i - 1)
                    v.bn_aggr(out=mv[0:R, i % 2, :], in_=stats[0:R, i % 2, :, :]).then_inc(S["n_mean"], 1)

                def apply(i):
                    R = ROWS[i]
                    v.wait_ge(S["n_rstd"], i + 1)
                    v.wait_ge(S["n_mean"], i + 1)
                    if i >= 2:
                        v.wait_ge(S["n_gained"], i - 1)
                    v.tensor_scalar(xn[0:R, i % 2, :], x[0:R, i % 3, :], mv[0:R, i % 2, 0:1], rs[0:R, i % 2, 1:2],
                                    ALU.subtract, ALU.mult).then_inc(S["n_scaled"], 1)

                def shift(i):
                    R = ROWS[i]
                    v.wait_ge(S["n_gained"], i + 1)
                    v.tensor_tensor(y[0:R, i % 3, :], y[0:R, i % 3, :], bias[0:R, :], ALU.add).then_inc(S["n_ready"], 1)

                v.wait_ge(S["n_const"], 48)
                for i in range(NT):
                    stats_of(i)
                    if i >= 1:
                        shift(i - 1)
                    apply(i)
                shift(NT - 1)
                for hc in range(HC):
                    v.wait_ge(S["n_comb"], hc + 1)
                    if hc >= 2:
                        v.wait_ge(S[f"n_wcst{hc % 2}"], 16 * (hc // 2))
                    for c in range(2):
                        last = v.tensor_copy(wc[:, hc % 2, 4 * c:4 * c + 4, :],
                                             ps[4 + 2 * (hc % 2) + c][:, :].rearrange("p (k n) -> p k n", k=4))
                    last.then_inc(S["n_combevac"], 1)

            @block.gpsimd
            def _(g):
                g.memset(half[:], -0.5).then_inc(S["n_g"], 1)
                g.wait_ge(S["n_const"], 48)
                for i in range(NT):
                    R = ROWS[i]
                    g.wait_ge(S["n_mean"], i + 1)
                    if i >= 2:
                        g.wait_ge(S["n_scaled"], i - 1)
                    g.tensor_scalar(rs[0:R, i % 2, 0:1], mv[0:R, i % 2, 1:2], LN_EPS, None, ALU.add).then_inc(S["n_g"], 1)
                    g.wait_ge(S["n_g"], i + 2)
                    g.tensor_tensor(rs[0:R, i % 2, 1:2], rs[0:R, i % 2, 0:1], half[0:R, :], ALU.pow).then_inc(S["n_rstd"], 1)
                    g.wait_ge(S["n_scaled"], i + 1)
                    if i >= 3:
                        g.wait_ge(S["n_tr"], 2 * (i - 2))
                        g.wait_ge(S[f"n_st{i % 3}"], 16 * (i // 3))
                    g.tensor_tensor(y[0:R, i % 3, :], xn[0:R, i % 2, :], gain[0:R, :], ALU.mult).then_inc(S["n_gained"], 1)

            @block.tensor
            def _(pe):
                def combine(hc):
                    pe.wait_ge(S[f"n_wq{hc % 3}"], 16 * (hc // 3 + 1))
                    if hc >= 2:
                        pe.wait_ge(S["n_combevac"], hc - 1)
                    for k in range(KT):
                        last = nc.tensor.matmul(ps[4 + 2 * (hc % 2) + k // 4][:, (k % 4) * NK:(k % 4 + 1) * NK],
                                                wq[:, hc % 3, k * P:(k + 1) * P], keys[:, hc, :], start=True, stop=True)
                    last.then_inc(S["n_comb"], 1)

                pe.wait_ge(S["n_const"], 48)
                pe.wait_ge(S["n_keysin"], 16)
                for i in range(NT):
                    R = ROWS[i]
                    pe.wait_ge(S["n_ready"], i + 1)
                    for c in range(2):
                        if i >= 2:
                            pe.wait_ge(S["n_evac"], 2 * (i - 2) + c + 1)
                        for k in range(4):
                            last = nc.tensor.transpose(ps[2 * (i % 2) + c][:, k * P:k * P + R],
                                                       y[0:R, i % 3, (4 * c + k) * P:(4 * c + k + 1) * P], ident[0:R, 0:R])
                        last.then_inc(S["n_tr"], 1)
                for hc in range(HC):
                    combine(hc)

            @block.scalar
            def _(act):
                act.dma_start(keys[:], io["keysT"][:, :, :]).then_inc(S["n_keysin"], 16)
                for b in range(3):
                    act.dma_start(wq[:, b, :], io["wqT"][:, b, :]).then_inc(S[f"n_wq{b}"], 16)
                for i in range(NT):
                    R = ROWS[i]
                    for c in range(2):
                        act.wait_ge(S["n_tr"], 2 * i + c + 1)
                        nc.scalar.copy(hT[:, 4 * c:4 * c + 4, COL0[i]:COL0[i] + R],
                                       ps[2 * (i % 2) + c][:, :].rearrange("p (k n) -> p k n", k=4)[:, :, 0:R]).then_inc(S["n_evac"], 1)
                for hc in range(HC):
                    act.wait_ge(S["n_combevac"], hc + 1)
                    act.dma_start(io["wc"][:, :, hc * NK:(hc + 1) * NK].rearrange("k p n -> p k n"),
                                  wc[:, hc % 2]).then_inc(S[f"n_wcst{hc % 2}"], 16)
                    if hc + 3 < HC:
                        act.dma_start(wq[:, hc % 3, :], io["wqT"][:, hc + 3, :]).then_inc(S[f"n_wq{hc % 3}"], 16)
                for b in range(2):
                    act.wait_ge(S[f"n_wcst{b}"], 16 * HC // 2)
        nc.all_engine_barrier(sems_to_clear=S.range)


def project_and_convolve(nc, io, hT, wA):
    HALF = PER // 2
    ctx = ExitStack()
    with ctx:
        sb = lambda n, s, d=F32: ctx.enter_context(nc.sbuf_tensor(n, s, d, allow_name_mangling=True))
        ident = sb("c_ident", [P, P])
        cbuf = sb("c_buf", [P, 2, SBUF_COLS])
        ybuf = sb("c_y", [P, 2, CONVW])
        sil = sb("c_sil", [P, 2, TOK])
        tok = sb("c_tok", [P, 2, TILES + 1, P])
        state_in = sb("c_state", [P, PER, DEC_B * CTX])
        state_out = sb("c_stateout", [P, PER, SEGS * CTX])
        cw = sb("c_w", [P, PER, TAPS + 1])
        ps = [ctx.enter_context(nc.psum_tensor(f"c_ps{i}", [P, 512], F32)) for i in range(8)]
        S = Signals(nc, ctx, ["c_w0", "c_w1", "c_cst", "c_ctx", "c_mm", "c_evac", "c_taps", "c_conv", "c_silu", "c_tr",
                              "c_trevac", "c_store0", "c_store1", "c_pool", "c_cs", "c_lastw"])
        with nc.Block() as block:
            @block.sync
            def _(sp):
                sp.dma_start(ident[:], io["ident"][:, :]).then_inc(S["c_cst"], 16)
                sp.wait_ge(S["c_cst"], 16)

            @block.gpsimd
            def _(g):
                for b in range(2):
                    g.memset(cbuf[:, b, PROMPT0:PROMPT0 + CTX], 0.0).then_inc(S["c_pool"], 1)
                g.wait_ge(S["c_pool"], 2)
        nc.all_engine_barrier(sems_to_clear=S.range)

        samples = lambda b: cbuf[:, b, 0:PROMPT0].rearrange("p (s t) -> p s t", s=DEC_B)
        with nc.Fori(0, CT // PER) as turn:
            with nc.Block() as block:
                @block.sync
                def _(sp):
                    W = HALF * P
                    sp.dma_start(wA[:, 1], io["w_in"][:, bass.ds(turn * (PER * P) + W, W)].rearrange(
                        "(k p) c -> p k c", p=P)).then_inc(S["c_w1"], 16)
                    sp.dma_start(cw[:], io["conv_w"][bass.ds(turn * PER, PER)].rearrange("j p c -> p j c")).then_inc(S["c_cst"], 16)
                    sp.dma_start(state_in[:], io["conv_in"][bass.ds(turn * PER, PER)].rearrange("j p c -> p j c")).then_inc(S["c_cst"], 16)
                    for j in range(PER):
                        sp.wait_ge(S["c_trevac"], 3 * (j + 1))
                        cols = bass.ds(turn * (PER * P) + j * P, P)
                        sp.dma_start(io["rows"][1:TILES + 1, :, cols].rearrange("i p c -> p i c"),
                                     tok[:, j % 2, 1:TILES + 1, :]).then_inc(S[f"c_store{j % 2}"], 16)
                        sp.dma_start(io["rows"][0, 0:PACK, cols], tok[0:PACK, j % 2, 0, :]).then_inc(S[f"c_store{j % 2}"], 16)
                        if j == HALF - 1:
                            sp.wait_ge(S["c_mm"], NCH * HALF)
                            sp.dma_start(wA[:, 0], io["w_in"][:, bass.ds(turn * (PER * P) + 2 * W, W)].rearrange(
                                "(k p) c -> p k c", p=P)).then_inc(S["c_lastw"], 16)
                    sp.wait_ge(S["c_pool"], 2 * PER)
                    sp.dma_start(io["conv_out"][bass.ds(turn * PER, PER)].rearrange("j p c -> p j c"), state_out[:]).then_inc(S["c_cs"], 16)
                    sp.wait_ge(S["c_cs"], 16)
                    sp.wait_ge(S["c_lastw"], 16)
                    for b in range(2):
                        sp.wait_ge(S[f"c_store{b}"], 32 * (PER // 2))

                @block.tensor
                def _(pe):
                    def transposes(j):
                        pe.wait_ge(S["c_silu"], j + 1)
                        for c in range(3):
                            n = 3 * j + c
                            if n >= 2:
                                pe.wait_ge(S["c_trevac"], n - 1)
                            tiles = [range(1, 5), range(5, 9), range(0, 1)][c]
                            for i in tiles:
                                last = nc.tensor.transpose(
                                    ps[6 + n % 2][0:ROWS[i], (i - tiles[0]) * P:(i - tiles[0] + 1) * P],
                                    sil[:, j % 2, COL0[i]:COL0[i] + ROWS[i]], ident[:, :])
                            last.then_inc(S["c_tr"], 1)

                    for j in range(PER):
                        if j == HALF:
                            pe.wait_ge(S["c_w1"], 16)
                        for c in range(NCH):
                            if j >= 2:
                                pe.wait_ge(S["c_evac"], NCH * (j - 2) + c + 1)
                            for k in range(KT):
                                last = nc.tensor.matmul(ps[NCH * (j % 2) + c][:, 0:NC_],
                                                        wA[:, j // HALF, k, (j % HALF) * P:(j % HALF + 1) * P],
                                                        hT[:, k, c * NC_:(c + 1) * NC_], start=(k == 0), stop=(k == KT - 1))
                            last.then_inc(S["c_mm"], 1)
                            if c == 1 and j >= 1:
                                transposes(j - 1)
                    transposes(PER - 1)

                @block.gpsimd
                def _(g):
                    g.wait_ge(S["c_cst"], 32)
                    for j in range(PER):
                        if j >= 2:
                            g.wait_ge(S["c_conv"], j - 1)
                            g.wait_ge(S["c_pool"], 2 * (j - 1))
                        g.tensor_copy(samples(j % 2)[:, :, 0:CTX],
                                      state_in[:, j, :].rearrange("p (s t) -> p s t", s=DEC_B)).then_inc(S["c_ctx"], 1)
                        g.wait_ge(S["c_evac"], NCH * (j + 1))
                        g.tensor_copy(state_out[:, j, 0:DEC_B * CTX].rearrange("p (s t) -> p s t", s=DEC_B),
                                      samples(j % 2)[:, :, DEC_L:SLOT]).then_inc(S["c_pool"], 1)
                        g.tensor_copy(state_out[:, j, DEC_B * CTX:SEGS * CTX],
                                      cbuf[:, j % 2, SBUF_COLS - CTX:SBUF_COLS]).then_inc(S["c_pool"], 1)

                @block.scalar
                def _(act):
                    def silu(j):
                        act.wait_ge(S["c_conv"], j + 1)
                        if j >= 2:
                            act.wait_ge(S["c_tr"], 3 * (j - 1))
                        y = ybuf[:, j % 2, :]
                        nc.scalar.activation(sil[:, j % 2, 0:SAMPLE].rearrange("p (s t) -> p s t", s=DEC_B),
                                             y[:, 0:PROMPT0].rearrange("p (s t) -> p s t", s=DEC_B)[:, :, 0:DEC_L], ACT.Silu)
                        nc.scalar.activation(sil[:, j % 2, SAMPLE:TOK], y[:, PROMPT0:PROMPT0 + TOK - SAMPLE],
                                             ACT.Silu).then_inc(S["c_silu"], 1)

                    for j in range(PER):
                        if j >= 2:
                            act.wait_ge(S["c_conv"], j - 1)
                            act.wait_ge(S["c_pool"], 2 * (j - 1))
                        for c in range(NCH):
                            act.wait_ge(S["c_mm"], NCH * j + c + 1)
                            bank = ps[NCH * (j % 2) + c]
                            skip = SAMPLE if c == 0 else 0
                            if c == 0:
                                nc.scalar.copy(samples(j % 2)[:, :, CTX:SLOT],
                                               bank[:, 0:SAMPLE].rearrange("p (s t) -> p s t", s=DEC_B))
                            to = PROMPT0 + CTX + c * NC_ + skip - SAMPLE
                            nc.scalar.copy(cbuf[:, j % 2, to:to + NC_ - skip], bank[:, skip:NC_]).then_inc(S["c_evac"], 1)
                            if c == 0 and j >= 1:
                                silu(j - 1)
                    silu(PER - 1)

                @block.vector
                def _(v):
                    def copy_out(j):
                        for c in range(3):
                            n = 3 * j + c
                            v.wait_ge(S["c_tr"], n + 1)
                            if j >= 2 and c == 0:
                                v.wait_ge(S[f"c_store{j % 2}"], 32 * (j // 2))
                            if c < 2:
                                v.tensor_copy(tok[:, j % 2, 1 + 4 * c:5 + 4 * c, :],
                                              ps[6 + n % 2][:, :].rearrange("p (i n) -> p i n", i=4)).then_inc(S["c_trevac"], 1)
                            else:
                                v.tensor_copy(tok[0:PACK, j % 2, 0, :], ps[6 + n % 2][0:PACK, 0:P]).then_inc(S["c_trevac"], 1)

                    taps = Chain(v, S["c_taps"])
                    v.wait_ge(S["c_cst"], 32)
                    for j in range(PER):
                        if j >= 1:
                            copy_out(j - 1)
                        v.wait_ge(S["c_evac"], NCH * (j + 1))
                        v.wait_ge(S["c_ctx"], j + 1)
                        if j >= 2:
                            v.wait_ge(S["c_silu"], j - 1)
                        x, y = cbuf[:, j % 2, :], ybuf[:, j % 2, :]
                        taps(v.tensor_scalar(y, x[:, 0:CONVW], cw[:, j, 0:1], cw[:, j, TAPS:TAPS + 1], ALU.mult, ALU.add))
                        for i in range(1, TAPS):
                            last = v.scalar_tensor_tensor(out=y, in0=x[:, i:i + CONVW], scalar=cw[:, j, i:i + 1], in1=y,
                                                          op0=ALU.mult, op1=ALU.add)
                            if i < TAPS - 1:
                                taps(last)
                        last.then_inc(S["c_conv"], 1)
                    copy_out(PER - 1)
            nc.all_engine_barrier(sems_to_clear=S.range)


def project_gates(nc, io, hT, small):
    ctx = ExitStack()
    with ctx:
        sb = lambda n, s, d=F32: ctx.enter_context(nc.sbuf_tensor(n, s, d, allow_name_mangling=True))
        NT = TILES + 1
        NCG = Z // ZC
        w = sb("z_w", [P, 2, KT, ZC])
        ws = sb("z_ws", [P, KT, SMALL])
        zs = sb("z_out", [P, 3, ZC])
        ps = [ctx.enter_context(nc.psum_tensor(f"z_ps{i}", [P, 512], F32)) for i in range(8)]
        S = Signals(nc, ctx, ["z_w0", "z_w1", "z_ws", "z_mm", "z_silu", "z_st0", "z_st1", "z_st2", "z_small", "z_zero"])
        with nc.Block() as block:
            @block.sync
            def _(sp):
                sp.dma_start(ws[:], io["w_in"][:, CONV + Z:CONV + Z + SMALL].rearrange("(k p) c -> p k c", p=P)).then_inc(S["z_ws"], 16)
                for g in range(NCG):
                    if g >= 2:
                        sp.wait_ge(S["z_mm"], NT * (g - 1))
                    sp.dma_start(w[:, g % 2], io["w_in"][:, CONV + g * ZC:CONV + (g + 1) * ZC].rearrange(
                        "(k p) c -> p k c", p=P)).then_inc(S[f"z_w{g % 2}"], 16)

            @block.tensor
            def _(pe):
                pe.wait_ge(S["z_ws"], 16)
                for i in range(NT):
                    for k in range(KT):
                        last = nc.tensor.matmul(ps[7][0:ROWS[i], i * SMALL:(i + 1) * SMALL],
                                                hT[:, k, COL0[i]:COL0[i] + ROWS[i]], ws[:, k, :], start=(k == 0), stop=(k == KT - 1))
                last.then_inc(S["z_small"], 1)
                for g in range(NCG):
                    pe.wait_ge(S[f"z_w{g % 2}"], 16 * (g // 2 + 1))
                    for i in range(NT):
                        n = NT * g + i
                        if n >= 6:
                            pe.wait_ge(S["z_silu"], n - 5)
                        for k in range(KT):
                            last = nc.tensor.matmul(ps[n % 6][0:ROWS[i], :], hT[:, k, COL0[i]:COL0[i] + ROWS[i]],
                                                    w[:, g % 2, k, :], start=(k == 0), stop=(k == KT - 1))
                        last.then_inc(S["z_mm"], 1)

            @block.scalar
            def _(act):
                for n in range(NCG * NT):
                    g, i = divmod(n, NT)
                    act.wait_ge(S["z_mm"], n + 1)
                    if n >= 3:
                        act.wait_ge(S[f"z_st{n % 3}"], 16 * (n // 3))
                    nc.scalar.activation(zs[0:ROWS[i], n % 3, :], ps[n % 6][0:ROWS[i], :], ACT.Silu).then_inc(S["z_silu"], 1)
                    act.wait_ge(S["z_silu"], n + 1)
                    act.dma_start(io["z"][i, 0:ROWS[i], g * ZC:(g + 1) * ZC], zs[0:ROWS[i], n % 3, :]).then_inc(S[f"z_st{n % 3}"], 16)
                for b in range(3):
                    act.wait_ge(S[f"z_st{b}"], 16 * len(range(b, NCG * NT, 3)))

            @block.gpsimd
            def _(g):
                g.memset(small[:, 0, :], 0.0).then_inc(S["z_zero"], 1)

            @block.vector
            def _(v):
                v.wait_ge(S["z_small"], 1)
                v.wait_ge(S["z_zero"], 1)
                v.tensor_copy(small[:, 1:NT, :], ps[7][:, SMALL:NT * SMALL].rearrange("p (i c) -> p i c", c=SMALL))
                v.tensor_copy(small[0:PACK, 0, :], ps[7][0:PACK, 0:SMALL]).then_inc(S["z_small"], 1)
        nc.all_engine_barrier(sems_to_clear=S.range)


def work_out_gates(nc, io, small, elast_pack):
    ctx = ExitStack()
    with ctx:
        sb = lambda n, s, d=F32: ctx.enter_context(nc.sbuf_tensor(n, s, d, allow_name_mangling=True))
        NT = TILES + 1
        upper, ones = sb("g_upper", [P, P]), sb("g_ones", [P, P])
        upper_seg, ones_seg, seg = sb("g_upseg", [PACK, PACK]), sb("g_onseg", [PACK, PACK]), sb("g_seg", [PACK, SEGS])
        bias, rate = sb("g_bias", [P, 2 * H]), sb("g_rate", [P, 2 * H])
        pre, mag, pos, sp_ = (sb(f"g_{n}", [P, NT, 2 * H]) for n in ("pre", "mag", "pos", "sp"))
        gseg = sb("g_gseg", [PACK, 2 * H, SEGS])
        out = sb("g_out", [P, NT, NG])
        ps = [ctx.enter_context(nc.psum_tensor(f"g_ps{i}", [P, 512], F32)) for i in range(4)]
        F = lambda n: out[:, :, GF[n][0]:GF[n][1]]
        S = Signals(nc, ctx, ["g_in", "g_v", "g_act", "g_zero", "g_decay", "g_sums", "g_store"])
        with nc.Block() as block:
            @block.sync
            def _(sp):
                for t, n in ((upper, "upper"), (ones, "ones"), (upper_seg, "upper_seg"), (ones_seg, "ones_seg"), (seg, "seg")):
                    sp.dma_start(t[:], io[n][:, :]).then_inc(S["g_in"], 16)
                sp.dma_start(bias[:], io["step_bias"][:, :].to_broadcast([P, 2 * H])).then_inc(S["g_in"], 16)
                sp.dma_start(rate[:], io["log_rate"][:, :].to_broadcast([P, 2 * H])).then_inc(S["g_in"], 16)

            @block.gpsimd
            def _(g):
                g.memset(out[:], 0.0).then_inc(S["g_zero"], 1)

            @block.vector
            def _(v):
                c = Chain(v, S["g_v"])
                v.wait_ge(S["g_in"], 16 * 7)
                v.wait_ge(S["g_zero"], 1)
                raw = small[:, :, H:3 * H]
                b32 = bias[:, :].unsqueeze(1).to_broadcast([P, NT, 2 * H])
                r32 = rate[:, :].unsqueeze(1).to_broadcast([P, NT, 2 * H])
                c(v.tensor_tensor(pre[:], raw, b32, ALU.add))
                c(v.scalar_tensor_tensor(out=mag[:], in0=pre[:], scalar=-1.0, in1=pre[:], op0=ALU.mult, op1=ALU.max))
                c(v.tensor_scalar(pos[:], pre[:], 0.0, None, ALU.max))
                v.wait_ge(S["g_act"], 2)
                c(v.tensor_scalar(mag[:], mag[:], 1.0, None, ALU.add))
                v.wait_ge(S["g_act"], 3)
                c(v.tensor_tensor(sp_[:], pos[:], mag[:], ALU.add))
                c(v.tensor_scalar(pre[:], sp_[:], -1.0, None, ALU.mult))
                v.tensor_tensor(F("g"), pre[:], r32, ALU.mult)
                c(v.tensor_copy(F("dt"), sp_[:, :, H:2 * H]))
                v.tensor_tensor(gseg[:], F("g")[0:PACK, 0, :].unsqueeze(2).to_broadcast([PACK, 2 * H, SEGS]),
                                seg[:, :].unsqueeze(1).to_broadcast([PACK, 2 * H, SEGS]), ALU.mult).then_inc(S["g_decay"], 1)
                v.wait_ge(S["g_sums"], 1)
                for i0, i1, R in ((1, NT, P), (0, 1, PACK)):
                    cum = ps[0 if i0 else 2][0:R, 0:(i1 - i0) * 2 * H].rearrange("p (i h) -> p i h", h=2 * H)
                    last = v.tensor_scalar(F("ncum")[0:R, i0:i1], cum, -1.0, None, ALU.mult)
                c(last)
                for i0, i1, R in ((1, NT, P), (0, 1, PACK)):
                    tot = ps[1 if i0 else 2][0:R, (0 if i0 else 2 * H):(0 if i0 else 2 * H) + (i1 - i0) * 2 * H].rearrange("p (i h) -> p i h", h=2 * H)
                    last = v.tensor_tensor(pos[0:R, i0:i1], tot, F("ncum")[0:R, i0:i1], ALU.add)
                c(last)
                v.wait_ge(S["g_act"], 5)
                v.tensor_copy(F("edl"), pre[:, :, 0:H])
                v.tensor_tensor(F("dtedl"), pre[:, :, H:2 * H], F("dt"), ALU.mult)
                c(v.scalar_tensor_tensor(out=F("nbecum"), in0=F("beta"), scalar=-1.0, in1=F("ecum")[:, :, 0:H], op0=ALU.mult, op1=ALU.mult))

            @block.tensor
            def _(pe):
                pe.wait_ge(S["g_decay"], 1)
                g = F("g")
                nc.tensor.matmul(ps[0][:, 0:TILES * 2 * H], upper[:], g[:, 1:NT, :], start=True, stop=True)
                nc.tensor.matmul(ps[1][:, 0:TILES * 2 * H], ones[:], g[:, 1:NT, :], start=True, stop=True)
                nc.tensor.matmul(ps[2][0:PACK, 0:2 * H], upper_seg[:], g[0:PACK, 0, :], start=True, stop=True)
                nc.tensor.matmul(ps[2][0:PACK, 2 * H:4 * H], ones_seg[:], g[0:PACK, 0, :], start=True, stop=True)
                nc.tensor.matmul(ps[3][:, 0:2 * H * SEGS], ones[0:PACK, :], gseg[:, :, :], start=True, stop=True).then_inc(S["g_sums"], 1)

            @block.scalar
            def _(act):
                act.wait_ge(S["g_v"], 3)
                nc.scalar.activation(mag[:], mag[:], ACT.Exp, scale=-1.0).then_inc(S["g_act"], 1)
                nc.scalar.activation(rate[:], rate[:], ACT.Exp).then_inc(S["g_act"], 1)
                act.wait_ge(S["g_v"], 4)
                nc.scalar.activation(mag[:], mag[:], ACT.Ln).then_inc(S["g_act"], 1)
                act.wait_ge(S["g_sums"], 1)
                act.wait_ge(S["g_v"], 9)
                for i0, i1, R in ((1, NT, P), (0, 1, PACK)):
                    n = (i1 - i0) * 2 * H
                    nc.scalar.activation(F("ecum")[0:R, i0:i1], ps[0 if i0 else 2][0:R, 0:n].rearrange("p (i h) -> p i h", h=2 * H), ACT.Exp)
                    nc.scalar.activation(pre[0:R, i0:i1], pos[0:R, i0:i1], ACT.Exp)
                nc.scalar.activation(F("elast")[:, 1:NT], ps[1][:, 0:TILES * 2 * H].rearrange("p (i h) -> p i h", h=2 * H), ACT.Exp)
                nc.scalar.activation(elast_pack[:], ps[3][:, 0:2 * H * SEGS].rearrange("p (h s) -> p h s", s=SEGS), ACT.Exp).then_inc(S["g_act"], 1)
                nc.scalar.activation(F("beta"), small[:, :, 0:H], ACT.Sigmoid).then_inc(S["g_act"], 1)
                act.wait_ge(S["g_v"], 10)
                act.wait_ge(S["g_act"], 5)
                act.dma_start(io["gates"][:, :, :].rearrange("i p c -> p i c"), out[:]).then_inc(S["g_store"], 16)
                act.wait_ge(S["g_store"], 16)
        nc.all_engine_barrier(sems_to_clear=S.range)


GROUP = 16
LAG = 20
NU, NV, NDIAG = 6, 6, 4
NW = 2
LEVELS, LEVELS_PACK = 7, 4
SUB = 4


class Uses:

    def __init__(self, S):
        self.S, self.count, self.of = S, {}, {}

    def add(self, bank, *key):
        self.count[bank] = self.count.get(bank, 0) + 1
        self.of[key] = (bank, self.count[bank])

    def open(self, pe, *key):
        bank, n = self.of[key]
        if n > 1:
            pe.wait_ge(self.S[f"free{bank}"], n - 1)
        return bank

    def filled(self, ins, *key):
        ins.then_inc(self.S[f"full{self.of[key][0]}"], 1)

    def ready(self, eng, *key):
        bank, n = self.of[key]
        eng.wait_ge(self.S[f"full{bank}"], n)
        return bank

    def read(self, ins, *key):
        ins.then_inc(self.S[f"free{self.of[key][0]}"], 1)

    def taken(self, eng, *key):
        bank, n = self.of[key]
        eng.wait_ge(self.S[f"free{bank}"], n)


def pe_order(U, packed):
    levels = LEVELS_PACK if packed else LEVELS
    for hf in range(2):
        for s in range(2):
            U.add(3 * s, "TRa", hf, s)
            U.add(3 * s + 1, "TRb", hf, s)
        for s in range(2):
            U.add(3 * s + 2, "CUM", hf, s)
            U.add(3 * s, "RAWa", hf, s)
            U.add(3 * s + 1, "RAWb", hf, s)
        for s in range(2):
            U.add(3 * s, "A", hf, s)
        for l in range(1, levels):
            for s in range(2):
                U.add(3 * s, "T", hf, s, l)
            for s in range(2):
                if l < levels - 1:
                    U.add(3 * s + 1, "X", hf, s, l)
                U.add(3 * s + 2, "XT", hf, s, l)
        if packed:
            for h in range(8 * hf, 8 * hf + 8):
                U.add(0, "KS", h)
                U.add(1, "QS", h)
        else:
            U.add(0, "KS", hf)
            U.add(1, "QS", hf)
        U.add(2, "DEL", hf)
        U.add(3, "PD", hf)
        if packed:
            U.add(2, "SUm", hf)
            for p in range(4 * hf, 4 * hf + 4):
                U.add(4 + p % 2, "SU", p)
        else:
            U.add(4, "SU", hf)
    U.add(5, "BCT")
    U.add(4, "CB")
    for sub in range(4):
        U.add(sub % 2, "CUMs", sub)
    for g in range(GROUPS):
        U.add(2 + g, "YI", g)
    if packed:
        for h in range(H):
            U.add(4 + h % 2, "YC", h)
        for g in range(GROUPS):
            U.add(g, "HUm", g)
        for h in range(H):
            U.add(h % 2, "HU", h)
    else:
        for g in range(GROUPS):
            U.add(4 + g, "YC", g)
            U.add(g, "HU", g)
    for i in range(4):
        U.add(i, "MT", i)
    for i in range(2):
        U.add(4 + i, "OUT", i)
    for i in range(2):
        U.add(i, "HT", i)
    for i in range(4):
        U.add(2 + i, "SC", i)


class Checkpoints:

    def __init__(self, weights, slots):
        total, at = float(sum(weights.values())), 0.0
        self.upto = {}
        for k, w in weights.items():
            at += w
            self.upto[k] = int(round(slots * at / total))


def checkpoint_weights():
    w = {"start": 3, "norm": 3, "prep": 3}
    for hf in range(2):
        w["raw", hf] = 2.5
        w["inv0", hf] = 2
        for l in range(1, LEVELS):
            w["T", hf, l] = 1.67
            w["X", hf, l] = 1.9
        w["r", hf] = 1
        w["o", hf] = 2.5
    for sub in range(4):
        w["M", sub] = 1.2
    for n in range(6):
        w["y", n] = 1.5
    w["mix"] = 4
    for n in range(8):
        w["w_out", n] = 1.2
    w["h1"] = 4
    for n in range(8):
        w["w_sc", n] = 1.2
    for hc in range(HC):
        w["top", hc] = 0.9
    w["cand"] = 2
    for h in range(EH):
        w["best", h] = 3.2 if h % 2 else 2.2
    return w


def allocate(nc, ctx):
    sb = lambda n, s, d=F32: ctx.enter_context(nc.sbuf_tensor(n, s, d, allow_name_mangling=True))
    B = {}
    for n, s, d in (
            ("ident", [P, P], F32), ("identb", [P, P], BF16), ("masks", [P, 8, P], F32), ("half", [P, 2 * H], F32),
            ("ssm_g", [P, D], F32), ("dn_g", [P, HD], F32), ("skip_D", [P, H], F32),
            ("ln1_g", [P, D], F32), ("ln1_b", [P, D], F32),
            ("iota", [P, TOPK], F32), ("skip", [P, 1], F32),
            ("S", [P, H // 2, P], F32), ("HT", [P, H * HD], F32),
            ("gt", [P, NG], F32), ("rows", [P, CONV], F32), ("z", [P, Z], F32), ("h", [P, D], F32),
            ("kqb", [P, 3 * H // 2, P], F32), ("dec", [P, 2, SUB, P], F32), ("atp", [P, 2, SUB, 2, P], F32),
            ("X", [P, 2, SUB, P], F32), ("XT", [P, 2, SUB, P], F32), ("T1", [P, 2, SUB, P], F32),
            ("kb_kdec", [P, 2 * D], F32), ("xdt", [P, 2, D], F32), ("r_tmp", [P, 2, 512], F32),
            ("delta", [P, 512], F32), ("bct", [P, 4, P], F32), ("cb", [P, 2, P], F32),
            ("ss", [P, 2 * H], F32), ("rs", [P, 2 * H], F32), ("ssy", [P, 2], F32), ("stats", [P, 2, 6], F32),
            ("mv", [P, 4], F32),
            ("top", [P, HC, TOPK], F32), ("topi", [P, HC, TOPK], U32),
            ("best", [P, EH, TOPK], F32), ("besti", [P, EH, TOPK], U32), ("half_i", [P, 2, EH * TOPK], U32),
            ("half_f", [P, 2, EH * TOPK], F32), ("pick", [P, 2, EH * TOPK], F32), ("norm", [P, 2, EH], F32),
            ("wbuf", [P, NW, 2 * D], F32), ("next_idx", [P, SLOTS], U32), ("next_gate", [P, SLOTS], F32)):
        B[n] = sb(n, s, d)
    B["r"], B["tmp"] = (B["r_tmp"][:, i, :] for i in range(2))
    B["sq"] = B["r_tmp"].rearrange("p i n -> p (i n)")
    return B


def weights_in(sp, io, B, n):
    dst, n = B["wbuf"][:, n % NW, :], n % 16
    if n < 8:
        return sp.dma_start(dst.rearrange("p (k c) -> p k c", k=2),
                            io["w_out"][n * 2 * P:(n + 1) * 2 * P, :].rearrange("(k p) c -> p k c", p=P))
    return sp.dma_start(dst, io["wc"][n - 8])


def mix_tile(nc, io, B, pool_dma, tile, R, packed, peer, elast_pack=None):
    ctx = ExitStack()
    with ctx:
        levels = LEVELS_PACK if packed else LEVELS
        sb = lambda n, s, d=F32: ctx.enter_context(nc.sbuf_tensor(n, s, d, allow_name_mangling=True))
        upper = sb("upper", [P, P])
        hidden = sb("hidden", [P, SUB, P], BF16)
        wbuf = B["wbuf"]
        if packed:
            seg, spk, hpk = sb("seg", [PACK, SEGS]), sb("spk", [P, H // 2, DEC_B, HD]), sb("hpk", [P, H, DEC_B, HD])
            own, by_seg = sb("own", [PACK, 2, DEC_B, HD]), sb("by_seg", [PACK, 2, DEC_B, HD])
            ks, qs = (B["T1"][0:PACK, i].rearrange("p h n -> p (h n)") for i in range(2))
            yc = B["sq"][0:PACK, :]
        bank = [ctx.enter_context(nc.psum_tensor(f"bank{i}", [P, 512], F32, allow_name_mangling=True)) for i in range(6)]
        names = [f"{a}{i}" for a in ("full", "free") for i in range(6)] + [
            "gates_in", "qk_in", "rows_in", "states_in", "z_in", "h_in", "consts", "w_in0", "w_in1", "w_used", "sumsq", "inv_norm", "qk_norm", "kb", "bv",
            "kdec", "xdt", "zg", "xskip", "inverse", "r_ready", "m_ready", "mix_ready", "h1_ready",
            "v", "g", "a", "o_sum", "y_sum", "o_rs", "y_rs", "h1_mean", "h1_rs", "seg_made", "soft",
            "exp_ready", "out_st"]
        S = Signals(nc, ctx, names + (peer.names if peer else []), pool_dma)
        U = Uses(S)
        pe_order(U, packed)
        if peer:
            peer.begin(nc, ctx, S)
        gt, rows, z, h = B["gt"], B["rows"], B["z"], B["h"]
        q, k, v_ = (rows[0:R, i * D:(i + 1) * D] for i in range(3))
        xs = rows[0:R, QKV:QKV + D]
        bcol = lambda g: rows[:, QKV + D + g * NST:QKV + D + (g + 1) * NST]
        ccol = lambda g: rows[:, QKV + D + (GROUPS + g) * NST:QKV + D + (GROUPS + g + 1) * NST]
        heads = lambda ap: ap.rearrange("p (h d) -> p h d", d=HD)
        F = lambda n, a=0, b=None: gt[:, GF[n][0] + a:(GF[n][1] if b is None else GF[n][0] + b)]
        per_head = lambda ap: bc_last(ap, HD)
        kb, kdec = B["kb_kdec"][:, 0:D], B["kb_kdec"][:, D:2 * D]
        scores = B["kb_kdec"]
        xdt, xdtl = B["xdt"][:, 0, :], B["xdt"][:, 1, :]
        o, y = q, k
        cand = rows[:, 0:2 * D].rearrange("p (h a b) -> p h a b", h=EH, a=TOPK)
        eq = rows[:, 2 * D:4 * D].rearrange("p (h a b) -> p h a b", h=EH, a=TOPK)
        mixT, h1T = B["kqb"][:, 0:16, :], B["kqb"][:, 16:24, :]
        gtile = lambda ap, n: ap[bass.ds(tile, 1)].rearrange("o p c -> p (o c)")[0:n]

        with nc.Block() as block:
            @block.sync
            def _(sp):
                sp.dma_start(rows[0:R, 0:2 * D], gtile(io["rows"], R)[:, 0:2 * D]).then_inc(S["qk_in"], 16)
                sp.dma_start(gt[0:P, :], gtile(io["gates"], P)).then_inc(S["gates_in"], 16)
                sp.dma_start(rows[0:R, 2 * D:CONV], gtile(io["rows"], R)[:, 2 * D:CONV]).then_inc(S["rows_in"], 16)
                sp.dma_start(upper[0:R, 0:R], io["upper_seg" if packed else "upper"][:, :]).then_inc(S["consts"], 16)
                sp.dma_start(B["delta"][0:R, 0:R], io["hidden_seg" if packed else "hidden"][:, :]).then_inc(S["consts"], 16)
                sp.dma_start(z[0:R, :], gtile(io["z"], R)).then_inc(S["z_in"], 16)
                sp.dma_start(h[0:R, :], gtile(io["h"], R)).then_inc(S["h_in"], 16)
                if packed:
                    sp.dma_start(seg[:], io["seg"][:, :]).then_inc(S["consts"], 16)
                    sp.dma_start(spk[:], io["dn_in"][:, :, :, :]).then_inc(S["states_in"], 16)
                    sp.dma_start(hpk[:], io["ssm_in"][:, :, :, :]).then_inc(S["states_in"], 16)
                for n in range(NW, 16 + NW):
                    if n - NW == 7:
                        U.ready(sp, "OUT", 1)
                    elif n - NW == 15:
                        U.ready(sp, "SC", 3)
                    else:
                        sp.wait_ge(S["w_used"], n - NW + (1 if n - NW < 7 else 0))
                    weights_in(sp, io, B, n).then_inc(S[f"w_in{n % NW}"], 16)
                if packed:
                    for p in range(H // 2 - 2, H // 2):
                        U.taken(sp, "SU", p)
                    sp.dma_start(io["dn_out"][:, :, :, :], spk[:]).then_inc(S["out_st"], 16)
                    for hh in range(H - 2, H):
                        U.taken(sp, "HU", hh)
                    sp.dma_start(io["ssm_out"][:, :, :, :], hpk[:]).then_inc(S["out_st"], 16)
                    sp.wait_ge(S["out_st"], 32)
                for i in range(NW):
                    sp.wait_ge(S[f"w_in{i}"], 16 * (16 // NW))
                if peer:
                    peer.sync(sp)

            @block.gpsimd
            def _(g):
                at = peer.pool(g) if peer else (lambda *a: None)
                c = Chain(g, S["g"])
                half = B["half"]

                def inverse_root(dst, src, scale, eps, done, n):
                    c(g.tensor_scalar(dst, src, scale, eps, ALU.mult, ALU.add))
                    g.tensor_tensor(dst, dst, half[0:R, 0:n], ALU.pow).then_inc(S[done], 1)

                at("start")
                g.wait_ge(S["consts"], 48 if packed else 32)
                for i in range(SUB):
                    c.mark(g.tensor_copy(hidden[0:R, i, 0:R], B["delta"][0:R, 0:R]))
                g.wait_ge(S["sumsq"], 1)
                inverse_root(B["rs"][0:R, :], B["ss"][0:R, :], 1.0, L2_EPS, "inv_norm", 2 * H)
                g.wait_ge(S["rows_in"], 16)
                g.wait_ge(S["gates_in"], 16)
                g.tensor_tensor(heads(v_), heads(v_), per_head(F("beta")[0:R]), ALU.mult).then_inc(S["bv"], 1)
                at("norm")
                at("prep")
                g.wait_ge(S["qk_norm"], 1)
                g.tensor_tensor(heads(kdec[0:R]), heads(k), per_head(F("edl")[0:R]), ALU.mult).then_inc(S["kdec"], 1)
                for hf in range(2):
                    at("raw", hf)
                    at("inv0", hf)
                    for l in range(1, LEVELS):
                        at("T", hf, l)
                        if hf == 0 and l == 1:
                            g.tensor_tensor(heads(xdt[0:R]), heads(xs), per_head(F("dt")[0:R]), ALU.mult).then_inc(S["xdt"], 1)
                        if hf == 0 and l == 2:
                            g.tensor_tensor(heads(xdtl[0:R]), heads(xs), per_head(F("dtedl")[0:R]), ALU.mult).then_inc(S["xdt"], 1)
                        if hf == 0 and l == 3:
                            g.wait_ge(S["xdt"], 2)
                            g.tensor_tensor(heads(xs), heads(xs), per_head(B["skip_D"][0:R]), ALU.mult).then_inc(S["xskip"], 1)
                        if hf == 0 and l == 4:
                            g.wait_ge(S["z_in"], 16)
                            g.tensor_tensor(heads(z[0:R, 0:D]), heads(z[0:R, 0:D]), bc_mid(B["dn_g"][0:R, :], H),
                                            ALU.mult).then_inc(S["zg"], 1)
                        at("X", hf, l)
                    at("r", hf)
                    at("o", hf)
                for sub in range(4):
                    at("M", sub)
                g.wait_ge(S["o_sum"], 1)
                inverse_root(B["rs"][0:R, 0:H], B["ss"][0:R, 0:H], 1.0 / HD, RMS_EPS, "o_rs", H)
                for n in range(6):
                    at("y", n)
                g.wait_ge(S["y_sum"], 1)
                inverse_root(B["ssy"][0:R, 1:2], B["ssy"][0:R, 0:1], 1.0 / D, RMS_EPS, "y_rs", 1)
                at("mix")
                for n in range(8):
                    at("w_out", n)
                g.wait_ge(S["h1_mean"], 1)
                inverse_root(B["mv"][0:R, 2:3], B["mv"][0:R, 1:2], 1.0, LN_EPS, "h1_rs", 1)
                at("h1")
                for n in range(8):
                    at("w_sc", n)
                for hc in range(HC):
                    at("top", hc)
                at("cand")
                for e in range(EH):
                    at("best", e)
                if peer:
                    peer.pool_end(g)

            @block.tensor
            def _(pe):
                at = peer.tensor(pe) if peer else (lambda *a: None)
                ident, identb = B["ident"], B["identb"]
                mm, tr = nc.tensor.matmul, nc.tensor.transpose
                atp, X, XT, T1, kqb = B["atp"], B["X"], B["XT"], B["T1"], B["kqb"]
                at("start")
                pe.wait_ge(S["qk_in"], 16)
                pe.wait_ge(S["rows_in"], 16)
                pe.wait_ge(S["gates_in"], 16)
                pe.wait_ge(S["consts"], 48 if packed else 32)
                pe.wait_ge(S["g"], SUB)
                at("norm")

                def cumulative(b, first):
                    mm(bank[b][0:R, :].rearrange("p (h n) -> p h n", h=SUB)[:, :, 0:R], identb[0:R, 0:R],
                       hidden[0:R, :, 0:R], start=True, stop=False, skip_group_check=True)
                    for i in range(SUB):
                        last = mm(bank[b][0:R, i * P:i * P + R], F("g", first + i, first + i + 1)[0:R].to_broadcast([R, R]),
                                  upper[0:R, 0:R], start=False, stop=True, skip_group_check=True)
                    return last

                for hf in range(2):
                    for s in range(2):
                        p0 = 4 * hf + 2 * s
                        if hf == 0 and s == 0:
                            pe.wait_ge(S["qk_norm"], 1)
                            pe.wait_ge(S["kb"], 1)
                        srcs = [(a, p) for p in (p0, p0 + 1) for a in (k, kb, q)]
                        for j0, j1, name in ((0, 4, "TRa"), (4, 6, "TRb")):
                            b = U.open(pe, name, hf, s)
                            for j in range(j0, j1):
                                a, p = srcs[j]
                                last = tr(bank[b][:, (j - j0) * P:(j - j0) * P + R], a[0:R, p * P:(p + 1) * P], ident[0:R, 0:R])
                            U.filled(last, name, hf, s)
                    if hf == 0:
                        at("prep")
                    for s in range(2):
                        first = 8 * hf + SUB * s
                        b = U.open(pe, "CUM", hf, s)
                        U.filled(cumulative(b, first), "CUM", hf, s)
                        for j, name in enumerate(("RAWa", "RAWb")):
                            U.taken(pe, "TRa", hf, s)
                            U.taken(pe, "TRb", hf, s)
                            b = U.open(pe, name, hf, s)
                            for i in range(2):
                                p = first // 2 + i
                                last = mm(bank[b][0:R, i * 2 * P:(i + 1) * 2 * P].rearrange("p (a n) -> p a n", a=2)[:, :, 0:R],
                                          kqb[j * HD:(j + 1) * HD, 3 * p, 0:R], kqb[j * HD:(j + 1) * HD, 3 * p + 1:3 * p + 3, 0:R],
                                          start=True, stop=True)
                            U.filled(last, name, hf, s)
                    at("raw", hf)
                    for s in range(2):
                        U.taken(pe, "RAWa", hf, s)
                        U.taken(pe, "RAWb", hf, s)
                        b = U.open(pe, "A", hf, s)
                        for i in range(SUB):
                            last = mm(bank[b][0:R, i * P:i * P + R], atp[0:R, s, i, 0, 0:R], ident[0:R, 0:R], start=True, stop=True)
                        U.filled(last, "A", hf, s)
                    at("inv0", hf)
                    for l in range(1, LEVELS):
                        if l < levels:
                            for s in range(2):
                                if l == 1:
                                    pe.wait_ge(S["inverse"], 2 * hf + s + 1)
                                else:
                                    U.taken(pe, "X", hf, s, l - 1)
                                    U.taken(pe, "XT", hf, s, l - 1)
                                b = U.open(pe, "T", hf, s, l)
                                for i in range(SUB):
                                    last = mm(bank[b][0:R, i * P:i * P + R], atp[0:R, s, i, 0, 0:R], X[0:R, s, i, 0:R], start=True, stop=True)
                                U.filled(last, "T", hf, s, l)
                        at("T", hf, l)
                        if l < levels:
                            for s in range(2):
                                U.taken(pe, "T", hf, s, l)
                                if l < levels - 1:
                                    b = U.open(pe, "X", hf, s, l)
                                    for i in range(SUB):
                                        last = mm(bank[b][0:R, i * P:i * P + R], XT[0:R, s, i, 0:R], T1[0:R, s, i, 0:R], start=True, stop=True)
                                    U.filled(last, "X", hf, s, l)
                                b = U.open(pe, "XT", hf, s, l)
                                for i in range(SUB):
                                    last = mm(bank[b][0:R, i * P:i * P + R], T1[0:R, s, i, 0:R], XT[0:R, s, i, 0:R], start=True, stop=True)
                                U.filled(last, "XT", hf, s, l)
                        at("X", hf, l)
                    if packed:
                        pe.wait_ge(S["states_in"], 32)
                        for hh in range(8 * hf, 8 * hf + 8):
                            p, j = hh // 2, hh % 2
                            for name, a in (("KS", 0), ("QS", 2)):
                                b = U.open(pe, name, hh)
                                U.filled(mm(bank[b][0:R, :], kqb[j * HD:(j + 1) * HD, 3 * p + a, 0:R],
                                            spk[j * HD:(j + 1) * HD, p, :, :], start=True, stop=True), name, hh)
                    else:
                        for name, a in (("KS", 0), ("QS", 2)):
                            b = U.open(pe, name, hf)
                            for i in range(4):
                                p = 4 * hf + i
                                last = mm(bank[b][0:R, i * P:(i + 1) * P], kqb[:, 3 * p + a, 0:R], B["S"][:, p, :], start=True, stop=True)
                            U.filled(last, name, hf)
                    at("r", hf)
                    pe.wait_ge(S["r_ready"], hf + 1)
                    for s in range(2):
                        U.taken(pe, "XT", hf, s, levels - 1)
                    b = U.open(pe, "DEL", hf)
                    for i in range(8):
                        last = mm(bank[b][0:R, i * HD:(i + 1) * HD], XT[0:R, i // SUB, i % SUB, 0:R], B["r"][0:R, i * HD:(i + 1) * HD],
                                  start=True, stop=True)
                    U.filled(last, "DEL", hf)
                    U.taken(pe, "DEL", hf)
                    b = U.open(pe, "PD", hf)
                    for i in range(8):
                        last = mm(bank[b][0:R, i * HD:(i + 1) * HD], atp[0:R, i // SUB, i % SUB, 1, 0:R],
                                  B["delta"][0:R, i * HD:(i + 1) * HD], start=True, stop=True)
                    U.filled(last, "PD", hf)
                    pe.wait_ge(S["kdec"], 1)
                    if packed:
                        b = U.open(pe, "SUm", hf)
                        for i in range(8):
                            hh, j = 8 * hf + i, i % 2
                            last = mm(bank[b][j * HD:(j + 1) * HD, (i // 2) * HD:(i // 2 + 1) * HD],
                                      kdec[SAMPLE:PACK, hh * HD:(hh + 1) * HD], B["delta"][SAMPLE:PACK, i * HD:(i + 1) * HD],
                                      start=True, stop=True)
                        U.filled(last, "SUm", hf)
                        for i in range(8):
                            hh, j = 8 * hf + i, i % 2
                            pe.wait_ge(S["seg_made"], hh + 1)
                            b = U.open(pe, "SU", hh // 2) if j == 0 else b
                            last = mm(bank[b][j * HD:(j + 1) * HD, :], kdec[0:R, hh * HD:(hh + 1) * HD], by_seg[0:R, i % 2, :, :],
                                      start=True, stop=True)
                            if j == 1:
                                U.filled(last, "SU", hh // 2)
                    else:
                        b = U.open(pe, "SU", hf)
                        for i in range(4):
                            last = mm(bank[b][:, i * P:(i + 1) * P], kdec[0:R, (4 * hf + i) * P:(4 * hf + i + 1) * P],
                                      B["delta"][0:R, i * P:(i + 1) * P], start=True, stop=True)
                        U.filled(last, "SU", hf)
                    at("o", hf)
                b = U.open(pe, "BCT")
                for j in range(4):
                    a = bcol(j) if j < 2 else ccol(j - 2)
                    last = tr(bank[b][:, j * P:j * P + R], a[0:R], ident[0:R, 0:R])
                U.filled(last, "BCT")
                U.taken(pe, "BCT")
                b = U.open(pe, "CB")
                for g in range(GROUPS):
                    last = mm(bank[b][0:R, g * P:g * P + R], B["bct"][:, g, 0:R], B["bct"][:, 2 + g, 0:R], start=True, stop=True)
                U.filled(last, "CB")

                def intra(sub):
                    pe.wait_ge(S["m_ready"], sub + 1)
                    if sub == 0:
                        pe.wait_ge(S["xdt"], 2)
                    if sub % 2 == 0:
                        U.open(pe, "YI", sub // 2)
                    for i in range(SUB):
                        hh = SUB * sub + i
                        last = mm(bank[2 + sub // 2][0:R, (hh % 8) * HD:(hh % 8 + 1) * HD], X[0:R, sub % 2, i, 0:R],
                                  xdt[0:R, hh * HD:(hh + 1) * HD], start=True, stop=True)
                    if sub % 2 == 1:
                        U.filled(last, "YI", sub // 2)

                for sub in range(4):
                    b = U.open(pe, "CUMs", sub)
                    U.filled(cumulative(b, H + SUB * sub), "CUMs", sub)
                    if sub >= 1:
                        intra(sub - 1)
                    at("M", sub)
                intra(3)
                if packed:
                    for hh in range(H):
                        b = U.open(pe, "YC", hh)
                        U.filled(mm(bank[b][0:R, :], B["bct"][:, 2 + hh // 8, 0:R], hpk[:, hh, :, :], start=True, stop=True), "YC", hh)
                    for g in range(GROUPS):
                        b = U.open(pe, "HUm", g)
                        U.filled(mm(bank[b][:, :], bcol(g)[SAMPLE:PACK], xdtl[SAMPLE:PACK, g * 512:(g + 1) * 512],
                                    start=True, stop=True), "HUm", g)
                    for hh in range(H):
                        pe.wait_ge(S["seg_made"], H + hh + 1)
                        b = U.open(pe, "HU", hh)
                        U.filled(mm(bank[b][:, :], bcol(hh // 8)[0:R], by_seg[0:R, hh % 2, :, :], start=True, stop=True), "HU", hh)
                else:
                    for g in range(GROUPS):
                        if g == 1:
                            for n in range(2):
                                at("y", n)
                        b = U.open(pe, "YC", g)
                        U.filled(mm(bank[b][0:R, :], B["bct"][:, 2 + g, 0:R], B["HT"][:, g * 512:(g + 1) * 512],
                                    start=True, stop=True), "YC", g)
                        b = U.open(pe, "HU", g)
                        U.filled(mm(bank[b][:, :], bcol(g)[0:R], xdtl[0:R, g * 512:(g + 1) * 512], start=True, stop=True), "HU", g)
                for n in range(6):
                    at("y", n)
                for i in range(4):
                    pe.wait_ge(S["mix_ready"], 1 + i // 2)
                    b = U.open(pe, "MT", i)
                    for j in range(4):
                        last = tr(bank[b][:, j * P:j * P + R], rows[0:R, (4 * i + j) * P:(4 * i + j + 1) * P], ident[0:R, 0:R])
                    U.filled(last, "MT", i)
                at("mix")
                for i in range(2):
                    U.open(pe, "OUT", i)
                for n in range(8):
                    if n >= NW:
                        pe.wait_ge(S[f"w_in{n % NW}"], 16 * (n // NW))
                    if n % 2 == 0:
                        U.taken(pe, "MT", n // 2)
                    for kk in range(2):
                        for i in range(2):
                            last = mm(bank[4 + i][0:R, :], mixT[:, 2 * n + kk, 0:R],
                                      wbuf[:, n % NW, kk * D + i * 512:kk * D + (i + 1) * 512],
                                      start=(n == 0 and kk == 0), stop=(n == 7 and kk == 1))
                            if n == 7 and kk == 1 and i == 0:
                                U.filled(last, "OUT", 0)
                    if n < 7:
                        last.then_inc(S["w_used"], 1)
                    else:
                        U.filled(last, "OUT", 1)
                    at("w_out", n)
                pe.wait_ge(S["h1_ready"], 1)
                for i in range(2):
                    b = U.open(pe, "HT", i)
                    for j in range(4):
                        last = tr(bank[b][:, j * P:j * P + R], h[0:R, (4 * i + j) * P:(4 * i + j + 1) * P], ident[0:R, 0:R])
                    if i == 1:
                        U.filled(last, "HT", i)
                    else:
                        U.filled(last, "HT", i)
                at("h1")
                for i in range(4):
                    U.open(pe, "SC", i)
                for n in range(8):
                    pe.wait_ge(S[f"w_in{n % NW}"], 16 * ((n + 8) // NW))
                    U.taken(pe, "HT", n // 4)
                    for i in range(4):
                        last = mm(bank[2 + i][0:R, :], h1T[:, n, 0:R], wbuf[:, n % NW, i * 512:(i + 1) * 512],
                                  start=(n == 0), stop=(n == 7))
                        if n == 7:
                            U.filled(last, "SC", i)
                    if n < 7:
                        last.then_inc(S["w_used"], 1)
                    at("w_sc", n)
                for hc in range(HC):
                    at("top", hc)
                at("cand")
                for e in range(EH):
                    at("best", e)
                if peer:
                    peer.tensor_end(pe)

            @block.scalar
            def _(act):
                at = peer.scalar(act) if peer else (lambda *a: None)
                cp = nc.scalar.copy
                view = lambda ap, n: ap.rearrange("p (j n) -> p j n", n=P)
                at("start")
                at("norm")
                act.wait_ge(S["gates_in"], 16)

                def decays(s, first):
                    for i in range(SUB):
                        last = nc.scalar.activation(B["dec"][0:R, s, i, 0:R], bank_now[0:R, i * P:i * P + R], ACT.Exp,
                                                    bias=F("ncum", first + i, first + i + 1)[0:R])
                    return last

                for hf in range(2):
                    for s in range(2):
                        p0 = 4 * hf + 2 * s
                        b = U.ready(act, "TRa", hf, s)
                        U.read(cp(B["kqb"][:, 3 * p0:3 * p0 + 4, 0:R], view(bank[b][:, :], 4)[:, :, 0:R]), "TRa", hf, s)
                        b = U.ready(act, "TRb", hf, s)
                        U.read(cp(B["kqb"][:, 3 * p0 + 4:3 * p0 + 6, 0:R], view(bank[b][:, 0:2 * P], 2)[:, :, 0:R]), "TRb", hf, s)
                    if hf == 0:
                        at("prep")
                    for s in range(2):
                        if hf == 1:
                            U.taken(act, "RAWa", 0, s)
                            U.taken(act, "RAWb", 0, s)
                        bank_now = bank[U.ready(act, "CUM", hf, s)]
                        U.read(decays(s, 8 * hf + SUB * s), "CUM", hf, s)
                    at("raw", hf)
                    at("inv0", hf)
                    for l in range(1, LEVELS):
                        at("T", hf, l)
                        at("X", hf, l)
                    at("r", hf)
                    b = U.ready(act, "DEL", hf)
                    if packed and hf == 1:
                        act.wait_ge(S["seg_made"], 8)
                    U.read(cp(B["delta"][0:R, :], bank[b][0:R, :]), "DEL", hf)
                    at("o", hf)
                b = U.ready(act, "BCT")
                U.read(cp(B["bct"][:, :, 0:R], view(bank[b][:, :], 4)[:, :, 0:R]), "BCT")
                b = U.ready(act, "CB")
                U.read(cp(B["cb"][0:R, :, 0:R], view(bank[b][0:R, 0:2 * P], 2)[:, :, 0:R]), "CB")
                for sub in range(4):
                    if sub < 2:
                        U.taken(act, "RAWb", 1, sub)
                    else:
                        act.wait_ge(S["m_ready"], sub - 1)
                    bank_now = bank[U.ready(act, "CUMs", sub)]
                    U.read(decays(sub % 2, H + SUB * sub), "CUMs", sub)
                    at("M", sub)
                for n in range(6):
                    at("y", n)
                for i in range(4):
                    b = U.ready(act, "MT", i)
                    U.read(cp(mixT[:, 4 * i:4 * i + 4, 0:R], view(bank[b][:, :], 4)[:, :, 0:R]), "MT", i)
                at("mix")
                for n in range(8):
                    at("w_out", n)
                for i in range(2):
                    b = U.ready(act, "HT", i)
                    U.read(cp(h1T[:, 4 * i:4 * i + 4, 0:R], view(bank[b][:, :], 4)[:, :, 0:R]), "HT", i)
                at("h1")
                for n in range(8):
                    at("w_sc", n)
                for i in range(4):
                    b = U.ready(act, "SC", i)
                    U.read(cp(scores[0:R, i * 512:(i + 1) * 512], bank[b][0:R, :]), "SC", i)
                for hc in range(HC):
                    at("top", hc)
                at("cand")
                for e in range(EH):
                    at("best", e)
                act.wait_ge(S["soft"], 1)
                nc.scalar.activation(B["best"][0:R], B["best"][0:R], ACT.Exp).then_inc(S["exp_ready"], 1)
                if peer:
                    peer.scalar_end(act)

            @block.vector
            def _(v):
                at = peer.vector(v) if peer else (lambda *a: None)
                c = Chain(v, S["v"])
                tt = v.tensor_tensor
                masks, ident = B["masks"], B["ident"]
                atp, X, XT, T1, sq, tmp, dec = B["atp"], B["X"], B["XT"], B["T1"], B["sq"], B["tmp"], B["dec"]
                mask = lambda l: bc_mid(masks[0:R, l, 0:R], SUB)
                heads4 = lambda b: bank[b][0:R, :].rearrange("p (h n) -> p h n", h=SUB)[:, :, 0:R]
                at("start")
                v.wait_ge(S["qk_in"], 16)
                c(tt(sq[0:R, :], q, q, ALU.mult))
                c(v.tensor_reduce(out=B["ss"][0:R, 0:H], in_=heads(sq[0:R, :]), axis=AX, op=ALU.add))
                c(tt(sq[0:R, :], k, k, ALU.mult))
                v.tensor_reduce(out=B["ss"][0:R, H:2 * H], in_=heads(sq[0:R, :]), axis=AX, op=ALU.add).then_inc(S["sumsq"], 1)
                at("norm")
                v.wait_ge(S["inv_norm"], 1)
                c(v.tensor_scalar(B["rs"][0:R, 0:H], B["rs"][0:R, 0:H], HD ** -0.5, None, ALU.mult))
                tt(heads(q), heads(q), per_head(B["rs"][0:R, 0:H]), ALU.mult)
                tt(heads(k), heads(k), per_head(B["rs"][0:R, H:2 * H]), ALU.mult).then_inc(S["qk_norm"], 1)
                v.wait_ge(S["qk_norm"], 1)
                v.wait_ge(S["gates_in"], 16)
                tt(heads(kb[0:R]), heads(k), per_head(F("beta")[0:R]), ALU.mult).then_inc(S["kb"], 1)
                at("prep")
                v.wait_ge(S["rows_in"], 16)
                v.wait_ge(S["consts"], 48 if packed else 32)
                for hf in range(2):
                    for s in range(2):
                        U.taken(v, "CUM", hf, s)
                        for j, name in enumerate(("RAWa", "RAWb")):
                            b = U.ready(v, name, hf, s)
                            for i in range(2):
                                last = tt(atp[0:R, s, 2 * i + j, :, 0:R],
                                          bank[b][0:R, i * 2 * P:(i + 1) * 2 * P].rearrange("p (a n) -> p a n", a=2)[:, :, 0:R],
                                          bc_mid(dec[0:R, s, 2 * i + j, 0:R], 2), ALU.mult)
                            U.read(last, name, hf, s)
                    at("raw", hf)
                    for s in range(2):
                        b = U.ready(v, "A", hf, s)
                        U.read(tt(T1[0:R, s, :, 0:R], heads4(b), mask(0), ALU.mult), "A", hf, s)
                        c(tt(XT[0:R, s, :, 0:R], atp[0:R, s, :, 0, 0:R], mask(7), ALU.mult))
                        tt(X[0:R, s, :, 0:R], T1[0:R, s, :, 0:R], bc_mid(ident[0:R, 0:R], SUB), ALU.add)
                        tt(XT[0:R, s, :, 0:R], XT[0:R, s, :, 0:R], bc_mid(ident[0:R, 0:R], SUB), ALU.add).then_inc(S["inverse"], 1)
                    at("inv0", hf)
                    for l in range(1, LEVELS):
                        if l < levels:
                            for s in range(2):
                                b = U.ready(v, "T", hf, s, l)
                                U.read(tt(T1[0:R, s, :, 0:R], heads4(b), mask(l), ALU.mult), "T", hf, s, l)
                        at("T", hf, l)
                        if l < levels:
                            for s in range(2):
                                if l < levels - 1:
                                    b = U.ready(v, "X", hf, s, l)
                                    U.read(tt(X[0:R, s, :, 0:R], X[0:R, s, :, 0:R], heads4(b), ALU.add), "X", hf, s, l)
                                b = U.ready(v, "XT", hf, s, l)
                                U.read(tt(XT[0:R, s, :, 0:R], XT[0:R, s, :, 0:R], heads4(b), ALU.add), "XT", hf, s, l)
                        at("X", hf, l)
                    if packed:
                        v.wait_ge(S["states_in"], 32)
                        for hh in range(8 * hf, 8 * hf + 8):
                            for name, to, n in (("KS", ks, 0), ("QS", qs, 1)):
                                b = U.ready(v, name, hh)
                                U.read(tt(own[:, n], bank[b][0:R, :].rearrange("p (s d) -> p s d", s=DEC_B),
                                          bc_last(seg[:, 0:DEC_B], HD), ALU.mult), name, hh)
                                U.taken(v, name, hh)
                                last = v.tensor_reduce(out=to[:, (hh % 8) * HD:(hh % 8 + 1) * HD],
                                                       in_=own[:, n].rearrange("p s d -> p d s"), axis=AX, op=ALU.add)
                        c(last)
                        ksrc, qsrc = ks, qs
                    else:
                        ksrc = bank[U.ready(v, "KS", hf)][0:R, :]
                    last = tt(heads(tmp[0:R, :]), heads(ksrc), per_head(F("nbecum", 8 * hf, 8 * hf + 8)[0:R]), ALU.mult)
                    if packed:
                        c(last)
                    else:
                        U.read(last, "KS", hf)
                        U.taken(v, "KS", hf)
                    if hf == 0:
                        v.wait_ge(S["bv"], 1)
                    tt(B["r"][0:R, :], v_[:, 512 * hf:512 * hf + 512], tmp[0:R, :], ALU.add).then_inc(S["r_ready"], 1)
                    at("r", hf)
                    if not packed:
                        qsrc = bank[U.ready(v, "QS", hf)][0:R, :]
                    oh = o[:, 512 * hf:512 * hf + 512]
                    last = tt(heads(oh), heads(qsrc), per_head(F("ecum", 8 * hf, 8 * hf + 8)[0:R]), ALU.mult)
                    if packed:
                        c(last)
                    else:
                        U.read(last, "QS", hf)
                        U.taken(v, "QS", hf)
                    b = U.ready(v, "PD", hf)
                    U.read(tt(oh, oh, bank[b][0:R, :], ALU.add), "PD", hf)
                    St = B["S"]
                    if packed:
                        b = U.ready(v, "SUm", hf)
                        for j in range(2):
                            sl = slice(j * HD, (j + 1) * HD)
                            last = v.tensor_copy(St[sl, 4 * hf:4 * hf + 4, j * HD:(j + 1) * HD],
                                                 bank[b][sl, 0:4 * HD].rearrange("p (a d) -> p a d", a=4))
                        U.read(last, "SUm", hf)
                        U.taken(v, "DEL", hf)
                        for p in range(4 * hf, 4 * hf + 4):
                            for j in range(2):
                                i = 2 * (p % 4) + j
                                if p >= 1:
                                    U.ready(v, "SU", p - 1)
                                tt(by_seg[0:R, j], B["delta"][0:R, i * HD:(i + 1) * HD].unsqueeze(1).to_broadcast([R, DEC_B, HD]),
                                   bc_last(seg[:, 0:DEC_B], HD), ALU.mult).then_inc(S["seg_made"], 1)
                            for j in range(2):
                                sl = slice(j * HD, (j + 1) * HD)
                                last = tt(spk[sl, p], spk[sl, p], bc_last(elast_pack[sl, 2 * p + j, 0:DEC_B], HD), ALU.mult)
                            c(last)
                            b = U.ready(v, "SU", p)
                            U.read(tt(spk[:, p], spk[:, p], bank[b][:, :].rearrange("p (s d) -> p s d", s=DEC_B), ALU.add), "SU", p)
                    else:
                        for j in range(2):
                            sl = slice(j * HD, (j + 1) * HD)
                            diag = St[sl, 4 * hf:4 * hf + 4, j * HD:(j + 1) * HD]
                            el = F("elast", 8 * hf, 8 * hf + 8)[sl].rearrange("p (a j) -> p a j", j=2)[:, :, j]
                            last = tt(diag, diag, bc_last(el, HD), ALU.mult)
                        c(last)
                        b = U.ready(v, "SU", hf)
                        for j in range(2):
                            sl = slice(j * HD, (j + 1) * HD)
                            diag = St[sl, 4 * hf:4 * hf + 4, j * HD:(j + 1) * HD]
                            last = tt(diag, diag, bank[b][sl, :].rearrange("p (a c) -> p a c", a=4)[:, :, j * HD:(j + 1) * HD], ALU.add)
                        U.read(last, "SU", hf)
                    at("o", hf)
                U.taken(v, "PD", 1)
                c(tt(sq[0:R, :], o, o, ALU.mult))
                v.tensor_reduce(out=B["ss"][0:R, 0:H], in_=heads(sq[0:R, :]), axis=AX, op=ALU.add).then_inc(S["o_sum"], 1)
                for sub in range(4):
                    U.taken(v, "CUMs", sub)
                    if sub == 0:
                        U.taken(v, "CB")
                    tt(X[0:R, sub % 2, :, 0:R], dec[0:R, sub % 2, :, 0:R], bc_mid(B["cb"][0:R, sub // 2, 0:R], SUB),
                       ALU.mult).then_inc(S["m_ready"], 1)
                    at("M", sub)
                v.wait_ge(S["o_rs"], 1)
                c(tt(heads(o), heads(o), per_head(B["rs"][0:R, 0:H]), ALU.mult))
                v.wait_ge(S["zg"], 1)
                tt(o, o, z[0:R, 0:D], ALU.mult).then_inc(S["mix_ready"], 1)
                at("y", 0)
                HT = B["HT"]
                if packed:
                    for hh in range(H):
                        b = U.ready(v, "YC", hh)
                        U.read(tt(own[:, hh % 2], bank[b][0:R, :].rearrange("p (s d) -> p s d", s=DEC_B),
                                  bc_last(seg[:, 0:DEC_B], HD), ALU.mult), "YC", hh)
                        U.taken(v, "YC", hh)
                        last = v.tensor_reduce(out=yc[:, hh * HD:(hh + 1) * HD], in_=own[:, hh % 2].rearrange("p s d -> p d s"),
                                               axis=AX, op=ALU.add)
                    c(last)
                    for g in range(GROUPS):
                        b = U.ready(v, "HUm", g)
                        U.read(v.tensor_copy(HT[:, g * 512:(g + 1) * 512], bank[b][:, :]), "HUm", g)
                    for hh in range(H + 1):
                        if hh < H:
                            if hh < 2:
                                U.ready(v, "SU", 7)
                            else:
                                U.ready(v, "HU", hh - 2)
                            tt(by_seg[0:R, hh % 2], xdtl[0:R, hh * HD:(hh + 1) * HD].unsqueeze(1).to_broadcast([R, DEC_B, HD]),
                               bc_last(seg[:, 0:DEC_B], HD), ALU.mult).then_inc(S["seg_made"], 1)
                            c(tt(hpk[:, hh], hpk[:, hh], bc_last(elast_pack[:, H + hh, 0:DEC_B], HD), ALU.mult))
                        if hh >= 1:
                            b = U.ready(v, "HU", hh - 1)
                            U.read(tt(hpk[:, hh - 1], hpk[:, hh - 1], bank[b][:, :].rearrange("p (s d) -> p s d", s=DEC_B),
                                      ALU.add), "HU", hh - 1)
                for g in range(GROUPS):
                    yh = y[:, g * 512:(g + 1) * 512]
                    src = yc[:, g * 512:(g + 1) * 512] if packed else bank[U.ready(v, "YC", g)][0:R, :]
                    last = tt(heads(yh), heads(src), per_head(F("ecum", H + 8 * g, H + 8 * g + 8)[0:R]), ALU.mult)
                    if packed:
                        c(last)
                    else:
                        U.read(last, "YC", g)
                        c(tt(heads(HT[:, g * 512:(g + 1) * 512]), heads(HT[:, g * 512:(g + 1) * 512]),
                             per_head(F("elast", H + 8 * g, H + 8 * g + 8)), ALU.mult))
                        b = U.ready(v, "HU", g)
                        U.read(tt(HT[:, g * 512:(g + 1) * 512], HT[:, g * 512:(g + 1) * 512], bank[b][:, :], ALU.add), "HU", g)
                    b = U.ready(v, "YI", g)
                    U.read(tt(yh, yh, bank[b][0:R, :], ALU.add), "YI", g)
                    at("y", 1 + g)
                U.taken(v, "YI", 1)
                v.wait_ge(S["xskip"], 1)
                c(tt(y, y, xs, ALU.add))
                at("y", 3)
                v.wait_ge(S["z_in"], 16)
                c(tt(y, y, z[0:R, D:2 * D], ALU.mult))
                at("y", 4)
                v.tensor_tensor_reduce(out=sq[0:R, :], in0=y, in1=y, scale=1.0, scalar=0.0, op0=ALU.mult, op1=ALU.add,
                                       accum_out=B["ssy"][0:R, 0:1]).then_inc(S["y_sum"], 1)
                at("y", 5)
                v.wait_ge(S["y_rs"], 1)
                v.scalar_tensor_tensor(out=y, in0=y, scalar=B["ssy"][0:R, 1:2], in1=B["ssm_g"][0:R, :], op0=ALU.mult,
                                       op1=ALU.mult).then_inc(S["mix_ready"], 1)
                at("mix")
                for n in range(8):
                    at("w_out", n)
                v.wait_ge(S["h_in"], 16)
                for i in range(2):
                    b = U.ready(v, "OUT", i)
                    U.read(v.scalar_tensor_tensor(out=h[0:R, i * 512:(i + 1) * 512], in0=h[0:R, i * 512:(i + 1) * 512],
                                                  scalar=ALPHA, in1=bank[b][0:R, :], op0=ALU.mult, op1=ALU.add), "OUT", i)
                for i in range(2):
                    U.taken(v, "OUT", i)
                    last = v.bn_stats(out=B["stats"][0:R, i, :], in_=h[0:R, i * 512:(i + 1) * 512])
                c(last)
                v.bn_aggr(out=B["mv"][0:R, 0:2], in_=B["stats"][0:R]).then_inc(S["h1_mean"], 1)
                v.wait_ge(S["h1_mean"], 1)
                c(v.scalar_tensor_tensor(out=h[0:R, :], in0=h[0:R, :], scalar=B["mv"][0:R, 0:1], in1=B["ln1_g"][0:R, :],
                                         op0=ALU.subtract, op1=ALU.mult))
                v.wait_ge(S["h1_rs"], 1)
                v.scalar_tensor_tensor(out=h[0:R, :], in0=h[0:R, :], scalar=B["mv"][0:R, 2:3], in1=B["ln1_b"][0:R, :],
                                       op0=ALU.mult, op1=ALU.add).then_inc(S["h1_ready"], 1)
                at("h1")
                for n in range(8):
                    at("w_sc", n)
                top, topi = B["top"], B["topi"]
                for hc in range(HC):
                    U.taken(v, "SC", hc // 4)
                    sc = scores[0:R, hc * NK:(hc + 1) * NK]
                    c(v.max(out=top[0:R, hc, 0:8], in_=sc))
                    c(v.max_index(out=topi[0:R, hc, 0:8], in_max=top[0:R, hc, 0:8], in_values=sc))
                    c(v.match_replace(out=sc, in_to_replace=top[0:R, hc, 0:8], in_values=sc, imm_value=-3.0e38))
                    c(v.max(out=top[0:R, hc, 8:16], in_=sc))
                    last = v.max_index(out=topi[0:R, hc, 8:16], in_max=top[0:R, hc, 8:16], in_values=sc)
                    if hc == HC - 1:
                        c(last)
                    at("top", hc)
                t4 = top[0:R].rearrange("p (h c) a -> p h c a", c=2)
                c(tt(cand[0:R], t4[:, :, 0, :].unsqueeze(3).to_broadcast([R, EH, TOPK, TOPK]),
                     t4[:, :, 1, :].unsqueeze(2).to_broadcast([R, EH, TOPK, TOPK]), ALU.add))
                at("cand")
                best, besti = B["best"], B["besti"]
                topf = top
                v.tensor_copy(topf[0:R], topi[0:R])

                def choice(e0, e1):
                    hi, hf_, pick = B["half_i"], B["half_f"], B["pick"]
                    ks_ = slice(e0 * TOPK, e1 * TOPK)
                    n = e1 - e0
                    flat = besti[0:R, e0:e1].rearrange("p h k -> p (h k)")
                    v.tensor_scalar(hi[0:R, 0, ks_], flat, 4, None, ALU.logical_shift_right)
                    c(v.tensor_scalar(hi[0:R, 1, ks_], flat, TOPK - 1, None, ALU.bitwise_and))
                    c(v.tensor_copy(hf_[0:R, :, ks_], hi[0:R, :, ks_]))
                    tf = topf[0:R].rearrange("p (h c) a -> p h c a", c=2)
                    it = B["iota"][0:R, :].unsqueeze(1).unsqueeze(1).to_broadcast([R, n, TOPK, TOPK])
                    for j in range(2):
                        c.mark(tt(eq[0:R, j * n:(j + 1) * n],
                                  hf_[0:R, j, ks_].rearrange("p (h k) -> p h k", h=n).unsqueeze(3).to_broadcast([R, n, TOPK, TOPK]),
                                  it, ALU.is_equal))
                    c.sync()
                    for j in range(2):
                        last = tt(eq[0:R, j * n:(j + 1) * n], eq[0:R, j * n:(j + 1) * n],
                                  tf[:, e0:e1, j, :].unsqueeze(2).to_broadcast([R, n, TOPK, TOPK]), ALU.mult)
                    c(last)
                    last = v.tensor_reduce(out=pick[0:R, :, ks_], in_=rows[0:R, 2 * D:2 * D + 2 * n * TOPK * TOPK].rearrange("p (j k a) -> p j k a", j=2, a=TOPK),
                                           axis=AX, op=ALU.add)
                    c(last)
                    c(v.scalar_tensor_tensor(out=pick[0:R, 0, ks_], in0=pick[0:R, 0, ks_], scalar=float(NK), in1=pick[0:R, 1, ks_],
                                             op0=ALU.mult, op1=ALU.add))

                for e in range(EH):
                    cd = rows[0:R, e * TOPK * TOPK:(e + 1) * TOPK * TOPK]
                    c(v.max(out=best[0:R, e, 0:8], in_=cd))
                    c(v.max_index(out=besti[0:R, e, 0:8], in_max=best[0:R, e, 0:8], in_values=cd))
                    c(v.match_replace(out=cd, in_to_replace=best[0:R, e, 0:8], in_values=cd, imm_value=-3.0e38))
                    c(v.max(out=best[0:R, e, 8:16], in_=cd))
                    c(v.max_index(out=besti[0:R, e, 8:16], in_max=best[0:R, e, 8:16], in_values=cd))
                    if e == EH - 1:
                        norm = B["norm"]
                        c(v.tensor_copy(norm[0:R, 0, :], best[0:R, :, 0]))
                        tt(best[0:R], best[0:R], bc_last(norm[0:R, 0, :], TOPK), ALU.subtract).then_inc(S["soft"], 1)
                    if e % 2 == 1:
                        choice(e - 1, e + 1)
                    at("best", e)
                if peer:
                    peer.vector_end(v)
                pick = B["pick"]
                if packed:
                    c(v.tensor_scalar(pick[0:R, 0, :], pick[0:R, 0, :], B["skip"][0:R, :], None, ALU.add))
                v.wait_ge(S["exp_ready"], 1)
                c(v.tensor_reduce(out=norm[0:R, 0, :], in_=best[0:R], axis=AX, op=ALU.add))
                c(v.reciprocal(norm[0:R, 1, :], norm[0:R, 0, :]))
                c(tt(B["next_gate"][0:R, :].rearrange("p (h k) -> p h k", h=EH), best[0:R], bc_last(norm[0:R, 1, :], TOPK), ALU.mult))
                c(v.tensor_copy(B["next_idx"][0:R, :], pick[0:R, 0, :]))
                if peer:
                    peer.take_choice(v)
        nc.all_engine_barrier(sems_to_clear=S.range)


def load_constants(nc, io, B, pool_dma):
    ctx = ExitStack()
    with ctx:
        S = Signals(nc, ctx, ["k_in", "k_set"], pool_dma)
        with nc.Block() as block:
            @block.sync
            def _(sp):
                n = 0
                for name in ("ident", "masks", "iota", "skip"):
                    sp.dma_start(B[name][:], io[name][:]).then_inc(S["k_in"], 16)
                    n += 16
                for name, src, w in (("ssm_g", "ssm_norm_g", D), ("dn_g", "dn_norm_g", HD), ("skip_D", "ssm_D", H),
                                     ("ln1_g", "ln1_g", D), ("ln1_b", "ln1_b", D)):
                    sp.dma_start(B[name][:], io[src][:, :].to_broadcast([P, w])).then_inc(S["k_in"], 16)
                    n += 16
                for i in range(NW):
                    weights_in(sp, io, B, i).then_inc(S["k_in"], 16)
                    n += 16
                sp.wait_ge(S["k_in"], n)

            @block.gpsimd
            def _(g):
                g.memset(B["half"][:], -0.5).then_inc(S["k_set"], 1)
                g.memset(B["S"][:], 0.0).then_inc(S["k_set"], 1)
                g.memset(B["h"][:], 0.0).then_inc(S["k_set"], 1)
                g.memset(B["next_idx"][:], NEXP).then_inc(S["k_set"], 1)
                g.memset(B["next_gate"][:], 0.0).then_inc(S["k_set"], 1)
                g.wait_ge(S["k_in"], 16 * (9 + NW))
                g.tensor_copy(B["identb"][:], B["ident"][:]).then_inc(S["k_set"], 1)
                g.wait_ge(S["k_set"], 6)
        nc.all_engine_barrier(sems_to_clear=S.range)


class Experts:

    names = ["dot", "act_done", "weight", "diag", "v_used",
             "ff", "x_used", "y_chain", "y_mean", "y_root", "y_pre", "y_out", "taken"]

    def __init__(self, nc, ctx):
        sb = lambda n, s, d=F32: ctx.enter_context(nc.sbuf_tensor(n, s, d, allow_name_mangling=True))
        self.x, self.idx, self.gate = sb("e_x", [P, D]), sb("e_idx", [P, SLOTS], U32), sb("e_gate", [P, SLOTS])
        self.dots, self.acts, self.weights = (sb(f"e_{n}", [P, SLOTS]) for n in ("dots", "acts", "weights"))
        self.u, self.v = sb("e_u", [P, NU, D]), sb("e_v", [P, NV, D])
        self.diag = sb("e_diag", [P, NDIAG, P])
        self.gain, self.bias = sb("e_gain", [P, D]), sb("e_bias", [P, D])
        self.stats, self.mv, self.root = sb("e_stats", [P, 2, 6]), sb("e_mv", [P, 4]), sb("e_root", [P, 2])
        self.ff = [ctx.enter_context(nc.psum_tensor(f"e_ff{i}", [P, 512], F32)) for i in range(2)]

    def prepare(self, nc, io, B):
        ctx = ExitStack()
        with ctx:
            S = Signals(nc, ctx, ["p_in", "p_set"])
            with nc.Block() as block:
                @block.sync
                def _(sp):
                    sp.dma_start(self.gain[:], io["ln2_g"][:, :].to_broadcast([P, D])).then_inc(S["p_in"], 16)
                    sp.dma_start(self.bias[:], io["ln2_b"][:, :].to_broadcast([P, D])).then_inc(S["p_in"], 16)
                    sp.wait_ge(S["p_in"], 32)

                @block.gpsimd
                def _(g):
                    g.memset(self.u[:], 0.0).then_inc(S["p_set"], 1)
                    g.memset(self.v[:], 0.0).then_inc(S["p_set"], 1)
                    g.wait_ge(S["p_set"], 2)
            nc.all_engine_barrier(sems_to_clear=S.range)

    def take(self, nc, B):
        ctx = ExitStack()
        with ctx:
            S = Signals(nc, ctx, ["t_set"])
            with nc.Block() as block:
                @block.vector
                def _(v):
                    v.tensor_copy(self.x[:], B["h"][:]).then_inc(S["t_set"], 1)
                    v.tensor_copy(self.gate[:], B["next_gate"][:]).then_inc(S["t_set"], 1)
                    v.wait_ge(S["t_set"], 3)

                @block.gpsimd
                def _(g):
                    g.tensor_copy(self.idx[:], B["next_idx"][:]).then_inc(S["t_set"], 1)
            nc.all_engine_barrier(sems_to_clear=S.range)

    def bind(self, io, B, out, R, points):
        self.io, self.B, self.out, self.R, self.points = io, B, out, R, points
        return self

    def begin(self, nc, ctx, S):
        self.nc, self.S = nc, S

    def steps(self, emit, ahead=0):
        done = [0]
        total = SLOTS + LAG

        def at(*point):
            upto = total if not point else min(total, self.points.upto[point if len(point) > 1 else point[0]] + ahead)
            for n in range(done[0], upto):
                emit(n)
            done[0] = max(done[0], upto)
        return at

    def pool(self, g):
        S, io = self.S, self.io
        off = lambda k: bass.IndirectOffsetOnAxis(ap=self.idx[:, k:k + 1], axis=0)

        def slot(n):
            if n < SLOTS:
                if n >= NU:
                    g.wait_ge(S["dot"], n - NU + 1)
                g.indirect_dma_start(out=self.u[:, n % NU, :], out_offset=None, in_=io["peer_u"][:, :], in_offset=off(n),
                                     bounds_check=NEXP - 1, oob_is_err=False).then_inc(S[f"u_in{n % NU}"], 16)
            k = n - LAG
            if 0 <= k:
                if k >= NV:
                    g.wait_ge(S["v_used"], k - NV + 1)
                g.indirect_dma_start(out=self.v[:, k % NV, :], out_offset=None, in_=io["peer_v"][:, :], in_offset=off(k),
                                     bounds_check=NEXP - 1, oob_is_err=False).then_inc(S[f"v_in{k % NV}"], 16)
        self.pool_at = self.steps(slot, ahead=min(NU, NV))
        return self.pool_at

    def pool_end(self, g):
        self.pool_at()
        S = self.S
        for ring, n in (("u", NU), ("v", NV)):
            for i in range(n):
                g.wait_ge(S[f"{ring}_in{i}"], 16 * len(range(i, SLOTS, n)))
        nums = [S[f"{ring}_in{i}"].num for ring, n in (("u", NU), ("v", NV)) for i in range(n)]
        g.dma_reset(range(min(nums), max(nums) + 1))
        g.wait_ge(S["y_mean"], 1)
        g.tensor_scalar(self.root[:, 0:1], self.mv[:, 1:2], 1.0, LN_EPS, ALU.mult, ALU.add).then_inc(S["y_root"], 1)
        g.wait_ge(S["y_root"], 1)
        g.tensor_tensor(self.root[:, 1:2], self.root[:, 0:1], self.B["half"][:, 0:1], ALU.pow).then_inc(S["y_root"], 1)

    def vector(self, v):
        S = self.S

        def slot(n):
            if n < SLOTS:
                v.wait_ge(S[f"u_in{n % NU}"], 16 * (n // NU + 1))
                v.tensor_tensor_reduce(out=self.u[:, n % NU, :], in0=self.u[:, n % NU, :], in1=self.x[:], scale=1.0, scalar=0.0,
                                       op0=ALU.mult, op1=ALU.add, accum_out=self.dots[:, n:n + 1]).then_inc(S["dot"], 1)
            if n >= GROUP and n % GROUP == 2 and n < SLOTS + GROUP:
                e = n // GROUP - 1
                sl = slice(e * GROUP, (e + 1) * GROUP)
                v.wait_ge(S["act_done"], e + 1)
                v.tensor_tensor(self.weights[:, sl], self.acts[:, sl], self.gate[:, sl], ALU.mult).then_inc(S["weight"], 1)
        self.vector_at = self.steps(slot)
        return self.vector_at

    def vector_end(self, v):
        self.vector_at()
        S, x = self.S, self.x
        y = self.u[:, 0, :]
        c = Chain(v, S["y_chain"])
        v.wait_ge(S["dot"], SLOTS)
        v.wait_ge(S["ff"], 1)
        for i in range(2):
            last = v.scalar_tensor_tensor(out=y[:, i * 512:(i + 1) * 512], in0=x[:, i * 512:(i + 1) * 512], scalar=ALPHA,
                                          in1=self.ff[i][:, :], op0=ALU.mult, op1=ALU.add)
        last.then_inc(S["x_used"], 1)
        v.wait_ge(S["x_used"], 1)
        for i in range(2):
            last = v.bn_stats(out=self.stats[:, i, :], in_=y[:, i * 512:(i + 1) * 512])
        c(last)
        v.bn_aggr(out=self.mv[:, 0:2], in_=self.stats[:]).then_inc(S["y_mean"], 1)
        v.wait_ge(S["y_mean"], 1)
        c(v.scalar_tensor_tensor(out=y, in0=y, scalar=self.mv[:, 0:1], in1=self.gain[:], op0=ALU.subtract, op1=ALU.mult))
        v.wait_ge(S["y_root"], 2)
        v.scalar_tensor_tensor(out=y, in0=y, scalar=self.root[:, 1:2], in1=self.bias[:], op0=ALU.mult,
                               op1=ALU.add).then_inc(S["y_pre"], 1)

    def take_choice(self, v):
        S, B = self.S, self.B
        v.tensor_copy(self.gate[:], B["next_gate"][:]).then_inc(S["taken"], 1)
        v.wait_ge(S["y_root"], 2)
        v.tensor_copy(self.idx[:], B["next_idx"][:]).then_inc(S["taken"], 1)
        v.wait_ge(S["taken"], 3)

    def scalar(self, act):
        S, nc = self.S, self.nc

        def slot(n):
            if n >= GROUP and n % GROUP == 0:
                e = n // GROUP - 1
                if e < SLOTS // GROUP:
                    sl = slice(e * GROUP, (e + 1) * GROUP)
                    act.wait_ge(S["dot"], GROUP * (e + 1))
                    nc.scalar.activation(self.acts[:, sl], self.dots[:, sl], ACT.Gelu).then_inc(S["act_done"], 1)
            k = n - LAG
            if 0 <= k:
                act.wait_ge(S["weight"], k // GROUP + 1)
                if k >= NDIAG:
                    act.wait_ge(S["v_used"], k - NDIAG + 1)
                nc.scalar.activation(self.diag[:, k % NDIAG, :], self.B["ident"][:, :], ACT.Copy,
                                     scale=self.weights[:, k:k + 1]).then_inc(S["diag"], 1)
        self.scalar_at = self.steps(slot)
        return self.scalar_at

    def scalar_end(self, act, take=True):
        self.scalar_at()
        if take:
            act.wait_ge(self.S["h1_ready"], 1)
            act.wait_ge(self.S["x_used"], 1)
            self.nc.scalar.copy(self.x[:], self.B["h"][:]).then_inc(self.S["taken"], 1)

    def tensor(self, pe):
        S, nc = self.S, self.nc

        def slot(n):
            k = n - LAG
            if 0 <= k:
                pe.wait_ge(S[f"v_in{k % NV}"], 16 * (k // NV + 1))
                pe.wait_ge(S["diag"], k + 1)
                for i in range(2):
                    last = nc.tensor.matmul(self.ff[i][:, :], self.diag[:, k % NDIAG, :], self.v[:, k % NV, i * 512:(i + 1) * 512],
                                            start=(k == 0), stop=(k == SLOTS - 1), skip_group_check=True)
                last.then_inc(S["v_used" if k < SLOTS - 1 else "ff"], 1)
        self.tensor_at = self.steps(slot)
        return self.tensor_at

    def tensor_end(self, pe):
        self.tensor_at()

    def sync(self, sp):
        S = self.S
        sp.wait_ge(S["y_pre"], 1)
        sp.dma_start(self.out, self.u[0:self.R, 0, :]).then_inc(S["y_out"], 16)
        sp.wait_ge(S["y_out"], 16)


def experts_alone(nc, e, pool_dma):
    ctx = ExitStack()
    with ctx:
        S = Signals(nc, ctx, e.names, pool_dma)
        e.begin(nc, ctx, S)
        with nc.Block() as block:
            @block.gpsimd
            def _(g):
                e.pool(g)
                e.pool_end(g)

            @block.tensor
            def _(pe):
                e.tensor(pe)
                e.tensor_end(pe)

            @block.scalar
            def _(act):
                e.scalar(act)
                e.scalar_end(act, take=False)

            @block.vector
            def _(v):
                e.vector(v)
                e.vector_end(v)

            @block.sync
            def _(sp):
                e.sync(sp)
        nc.all_engine_barrier(sems_to_clear=S.range)


def store_states(nc, io, B):
    ctx = ExitStack()
    with ctx:
        S = Signals(nc, ctx, ["s_out"])
        with nc.Block() as block:
            @block.sync
            def _(sp):
                for j in range(2):
                    sl = slice(j * HD, (j + 1) * HD)
                    sp.dma_start(io["dn_out_p"][sl], B["S"][sl, :, j * HD:(j + 1) * HD]).then_inc(S["s_out"], 16)
                sp.dma_start(io["ssm_out_p"].rearrange("p h d -> p (h d)"), B["HT"][:]).then_inc(S["s_out"], 16)
                sp.wait_ge(S["s_out"], 48)
        nc.all_engine_barrier(sems_to_clear=S.range)


def program(nc, io):
    with ExitStack() as all_:
        names = [f"u_in{i}" for i in range(NU)] + [f"v_in{i}" for i in range(NV)]
        pool_dma = {n: all_.enter_context(nc.semaphore(n)) for n in names}
        elast_pack = all_.enter_context(nc.sbuf_tensor("elast_pack", [P, 2 * H, SEGS], F32))
        with ExitStack() as ctx:
            hT = ctx.enter_context(nc.sbuf_tensor("hT", [P, KT, TOK], F32))
            small = ctx.enter_context(nc.sbuf_tensor("small", [P, TILES + 1, SMALL], F32))
            with ExitStack() as c2:
                wA = c2.enter_context(nc.sbuf_tensor("wA", [P, 2, KT, PER // 2 * P], F32))
                normalize_and_combine_keys(nc, io, hT, wA)
                project_and_convolve(nc, io, hT, wA)
            project_gates(nc, io, hT, small)
            work_out_gates(nc, io, small, elast_pack)
        B = allocate(nc, all_)
        load_constants(nc, io, B, pool_dma)
        mix_tile(nc, io, B, pool_dma, 0, PACK, True, None, elast_pack=elast_pack)
        with ExitStack() as ctx:
            e = Experts(nc, ctx)
            points = Checkpoints(checkpoint_weights(), SLOTS + LAG)
            e.prepare(nc, io, B)
            e.take(nc, B)
            mix_tile(nc, io, B, pool_dma, 1, P, False, e.bind(io, B, io["y"][0:SAMPLE, :], SAMPLE, points))
            with nc.Fori(2, TILES + 1) as tile:
                mix_tile(nc, io, B, pool_dma, tile, P, False,
                         e.bind(io, B, io["y"][bass.ds(tile * P + (SAMPLE - 2 * P), P), :], P, points))
            e.bind(io, B, io["y"][SAMPLE + (TILES - 1) * P:SAMPLE + TILES * P, :], P, points)
            experts_alone(nc, e, pool_dma)
            store_states(nc, io, B)


def tables():
    i = np.arange(P)
    upper = (i[:, None] <= i[None, :]).astype(np.float32)
    seg_of = np.minimum(np.arange(PACK) // DEC_L, DEC_B)
    same = seg_of[:, None] == seg_of[None, :]
    upper_seg = upper[:PACK, :PACK] * same
    levels = []
    for l in range(7):
        block = (i[:, None] >> (l + 1)) == (i[None, :] >> (l + 1))
        low = block & (((i[:, None] >> l) & 1) == 1) & (((i[None, :] >> l) & 1) == 0)
        levels.append(-low.astype(np.float32))
    return {
        "ident": np.eye(P, dtype=np.float32),
        "ones": np.ones((P, P), np.float32),
        "upper": upper,
        "upper_seg": upper_seg.astype(np.float32),
        "ones_seg": same.astype(np.float32),
        "seg": (seg_of[:, None] == np.arange(SEGS)[None, :]).astype(np.float32),
        "masks": np.ascontiguousarray(np.stack(levels + [levels[0].T], axis=1)),
        "hidden": np.where(upper > 0, 0.0, NEG).astype(np.float32),
        "hidden_seg": np.where(upper_seg > 0, 0.0, NEG).astype(np.float32),
        "iota": np.ascontiguousarray(np.broadcast_to(np.arange(TOPK, dtype=np.float32), (P, TOPK))),
        "skip": np.where(i[:, None] >= SAMPLE, float(NEXP), 0.0).astype(np.float32),
    }


def layout(x):
    a = {k: np.asarray(v) for k, v in x.items()}
    d = {}
    d["x"] = np.concatenate([a["x_sample"].reshape(SAMPLE, D), a["meta_tokens"], a["x_prompt"].reshape(SEQ, D)], axis=0)
    w = a["w_in"][0]
    c = np.cumsum([0, QKV, H * HD, H, H, H * HD, XBC, H])
    qkv, zd, b, aa, zs, xbc, dt = (w[:, c[i]:c[i + 1]] for i in range(7))
    pad = np.zeros((D, 3 * P), np.float32)
    d["w_in"] = np.concatenate([qkv, xbc, zd, zs, b, aa, dt, pad], axis=1)
    taps = np.concatenate([a["dn_conv_w"][0], a["ssm_conv_w"][0]], axis=1)
    bias = np.concatenate([np.zeros((1, QKV), np.float32), a["ssm_conv_b"]], axis=1)
    d["conv_w"] = np.concatenate([taps, bias], axis=0).T.reshape(CT, P, TAPS + 1)
    st = np.concatenate([a["state_dn_conv"][0], a["state_ssm_conv"][0]], axis=2)
    d["conv_in"] = st.transpose(2, 0, 1).reshape(CT, P, DEC_B * CTX)
    s = a["state_dn_rec"][0].reshape(DEC_B, H // 2, 2, HD, HD)
    d["dn_in"] = s.transpose(2, 3, 1, 0, 4).reshape(P, H // 2, DEC_B, HD)
    d["ssm_in"] = a["state_ssm_rec"][0].transpose(3, 1, 0, 2)
    d["step_bias"] = np.concatenate([a["dn_dt_bias"], a["ssm_dt_bias"]], axis=1)
    d["log_rate"] = np.concatenate([a["dn_A_log"], a["ssm_A_log"]], axis=1)
    for n in ("ln_in_g", "ln_in_b", "ln1_g", "ln1_b", "ln2_g", "ln2_b", "ssm_norm_g"):
        d[n] = a[n].reshape(1, D)
    d["dn_norm_g"], d["ssm_D"] = a["dn_norm_g"].reshape(1, HD), a["ssm_D"].reshape(1, H)
    d["w_out"] = a["w_out"][0]
    d["wqT"] = a["peer_w_q"][0].reshape(D, HC, P).transpose(2, 1, 0)
    d["keysT"] = a["peer_keys"][0].reshape(HC, NK, P).transpose(2, 0, 1)
    d["peer_u"], d["peer_v"] = a["peer_u"][0], a["peer_v"][0]
    d.update(tables())
    return {k: np.ascontiguousarray(v) for k, v in d.items()}


OUTS = {
    "y": (SAMPLE + SEQ, D),
    "conv_out": (CT, P, SEGS * CTX),
    "dn_out": (P, H // 2, DEC_B, HD),
    "dn_out_p": (P, H // 2, HD),
    "ssm_out": (P, H, DEC_B, HD),
    "ssm_out_p": (P, H, HD),
}
SCRATCH = {
    "h": (TILES + 1, P, D),
    "rows": (TILES + 1, P, CONV),
    "z": (TILES + 1, P, Z),
    "gates": (TILES + 1, P, NG),
    "wc": (KT, P, HC * NK),
}


def results(r):
    y = r["y"]
    conv = r["conv_out"].reshape(CONV, SEGS, CTX).transpose(1, 2, 0)
    dn = r["dn_out"].reshape(2, HD, H // 2, DEC_B, HD).transpose(3, 2, 0, 1, 4).reshape(DEC_B, H, HD, HD)
    dn_p = r["dn_out_p"].reshape(2, HD, H // 2, HD).transpose(2, 0, 1, 3).reshape(1, H, HD, HD)
    ssm = r["ssm_out"].transpose(2, 1, 3, 0)
    ssm_p = r["ssm_out_p"].transpose(1, 2, 0)[None]
    out = (y[SAMPLE:].reshape(1, SEQ, D), y[:SAMPLE].reshape(DEC_B, DEC_L, D),
           conv[None, DEC_B:, :, :QKV], dn_p[None], conv[None, DEC_B:, :, QKV:], ssm_p[None],
           conv[None, :DEC_B, :, :QKV], dn[None], conv[None, :DEC_B, :, QKV:], ssm[None])
    return tuple(np.ascontiguousarray(o) for o in out)


def kernel(**inputs):
    import concourse.bacc as bacc
    from concourse.bass_utils import run_bass_kernel_spmd

    nc = bacc.Bacc("TRN2", target_bir_lowering=False, num_devices=1)
    arrays = layout(inputs)
    io = {n: nc.dram_tensor(n, a.shape, mybir.dt.from_np(a.dtype), kind="ExternalInput").ap() for n, a in arrays.items()}
    for n, s in OUTS.items():
        io[n] = nc.dram_tensor(n, s, F32, kind="ExternalOutput").ap()
    for n, s in SCRATCH.items():
        io[n] = nc.dram_tensor(n, s, F32, kind="Internal").ap()
    program(nc, io)
    r = run_bass_kernel_spmd(nc, [arrays], core_ids=[0])
    return results({n: r.results[0][n] for n in OUTS})
```
